# Optimizing a Trainium2 kernel written in Bass

```python
import math
import jax, jax.numpy as jnp
from jax import lax
import numpy as np

D_MODEL = 1024
BATCH = 1
SEQ = 1024
DEPTH = 2

CHUNK = 64
Q_BLOCK = 128
HEAD_DIM = 64
EPS = 1e-5
NEG = -1e30

A_HEADS = 4
A_V_DIM = 2 * HEAD_DIM
B_HEADS = 4
B_KV_HEADS = 2
B_GROUP = B_HEADS // B_KV_HEADS
B_WINDOW = 128
B_WIN_CHUNKS = B_WINDOW // CHUNK
C_HEADS = 4

N_ALIBI = A_HEADS + B_HEADS
D_MIX = A_HEADS * A_V_DIM + B_HEADS * HEAD_DIM + C_HEADS * HEAD_DIM
D_FF = 4 * D_MODEL

SPLIT_SIZES = (
    A_HEADS * 2 * HEAD_DIM,
    A_HEADS * 2 * HEAD_DIM,
    A_HEADS * A_V_DIM,
    B_HEADS * HEAD_DIM,
    B_KV_HEADS * HEAD_DIM,
    B_KV_HEADS * HEAD_DIM,
    C_HEADS * HEAD_DIM,
    C_HEADS * HEAD_DIM,
    C_HEADS * HEAD_DIM,
    C_HEADS,
)
D_IN = sum(SPLIT_SIZES)

kernel_name = "hybrid_diff_swa_sink_fox_block"

def rmsnorm(x, g):
    xf = x.astype(jnp.float32)
    y = xf * lax.rsqrt(jnp.mean(xf * xf, axis=-1, keepdims=True) + EPS)
    return (y * g.astype(jnp.float32)).astype(x.dtype)

def alibi_slopes():
    s = jnp.asarray([2.0 ** (-8.0 * (i + 1) / N_ALIBI) for i in range(N_ALIBI)], dtype=jnp.float32)
    return s[0::2], s[1::2]

def diff_attention(q, k, v, lam, lam_init, g_sub, slopes):
    B, S, H, _, d = q.shape
    scale = d ** -0.5
    outs = []
    for i in range(S // Q_BLOCK):
        q0 = i * Q_BLOCK
        kend = q0 + Q_BLOCK
        s = jnp.einsum('bqhmd,bkhmd->bhmqk', q[:, q0:kend], k[:, :kend]).astype(jnp.float32) * scale
        pos_q = jnp.arange(q0, kend)
        pos_k = jnp.arange(kend)
        dist = jnp.abs(pos_q[:, None] - pos_k[None, :]).astype(jnp.float32)
        allowed = (pos_k[None, :] // CHUNK) <= (pos_q[:, None] // CHUNK)
        s = jnp.where(allowed, s - slopes[:, None, None, None] * dist, NEG)
        p = jax.nn.softmax(s, axis=-1)
        a = p[:, :, 0] - lam * p[:, :, 1]
        outs.append(jnp.einsum('bhqk,bkhe->bqhe', a.astype(v.dtype), v[:, :kend]))
    o = jnp.concatenate(outs, axis=1)
    o = rmsnorm(o, g_sub) * (1.0 - lam_init)
    return o.reshape(B, S, H * v.shape[-1])

def sliding_window_sink_attention(q, k, v, sinks, slopes):
    B, S, Hkv, G, d = q.shape
    nb = S // Q_BLOCK
    scale = d ** -0.5
    qb = q.reshape(B, nb, Q_BLOCK, Hkv, G, d)

    def windows(t):
        tp = jnp.concatenate([jnp.zeros_like(t[:, :Q_BLOCK]), t], axis=1).reshape(B, nb + 1, Q_BLOCK, Hkv, d)
        return jnp.concatenate([tp[:, :-1], tp[:, 1:]], axis=2)

    kw = windows(k)
    vw = windows(v)
    s = jnp.einsum('bnqhgd,bnjhd->bnhgqj', qb, kw).astype(jnp.float32) * scale
    qi = jnp.arange(Q_BLOCK)
    j = jnp.arange(2 * Q_BLOCK)
    n = jnp.arange(nb)
    dchunk = (qi[:, None] + Q_BLOCK) // CHUNK - j[None, :] // CHUNK
    valid_key = (n[:, None] * Q_BLOCK - Q_BLOCK + j[None, :]) >= 0
    allowed = ((dchunk >= 0) & (dchunk < B_WIN_CHUNKS))[None] & valid_key[:, None, :]
    dist = jnp.abs(qi[:, None] + Q_BLOCK - j[None, :]).astype(jnp.float32)
    s = s - slopes.reshape(Hkv, G)[:, :, None, None] * dist
    s = jnp.where(allowed[:, None, None], s, NEG)
    sink = sinks.reshape(Hkv, G).astype(jnp.float32)[:, :, None, None]
    m = jnp.maximum(s.max(axis=-1, keepdims=True), sink)
    e = jnp.exp(s - m)
    p = e / (e.sum(axis=-1, keepdims=True) + jnp.exp(sink - m))
    o = jnp.einsum('bnhgqj,bnjhd->bnqhgd', p.astype(v.dtype), vw)
    return o.reshape(B, S, Hkv * G * d)

def forgetting_attention(q, k, v, log_f):
    B, S, H, d = q.shape
    scale = d ** -0.5
    cum = jnp.cumsum(log_f, axis=1).transpose(0, 2, 1)
    outs = []
    for i in range(S // Q_BLOCK):
        q0 = i * Q_BLOCK
        kend = q0 + Q_BLOCK
        s = jnp.einsum('bqhd,bkhd->bhqk', q[:, q0:kend], k[:, :kend]).astype(jnp.float32) * scale
        s = s + cum[:, :, q0:kend, None] - cum[:, :, None, :kend]
        pos_q = jnp.arange(q0, kend)
        pos_k = jnp.arange(kend)
        s = jnp.where(pos_k[None, :] <= pos_q[:, None], s, NEG)
        p = jax.nn.softmax(s, axis=-1)
        outs.append(jnp.einsum('bhqk,bkhd->bqhd', p.astype(v.dtype), v[:, :kend]))
    o = jnp.concatenate(outs, axis=1)
    return o.reshape(B, S, H * d)

def setup_inputs(seed: int = 0) -> dict:
    key = jax.random.key(seed)
    ks = jax.random.split(key, 13)
    nrm = jax.random.normal
    f32 = jnp.float32
    x = nrm(ks[0], (BATCH, SEQ, D_MODEL), f32)
    w_in = nrm(ks[1], (DEPTH, D_MODEL, D_IN), f32) * D_MODEL ** -0.5
    a_lambda = 0.1 * nrm(ks[2], (DEPTH, 4, HEAD_DIM), f32)
    a_subln = 1.0 + 0.02 * nrm(ks[3], (DEPTH, A_V_DIM), f32)
    b_sinks = 0.5 * nrm(ks[4], (DEPTH, B_HEADS), f32)
    c_fbias = 3.0 + 0.5 * nrm(ks[5], (DEPTH, C_HEADS), f32)
    w_out = nrm(ks[6], (DEPTH, D_MIX, D_MODEL), f32) * D_MIX ** -0.5
    g_mix = 1.0 + 0.02 * nrm(ks[7], (DEPTH, D_MODEL), f32)
    g_mlp = 1.0 + 0.02 * nrm(ks[8], (DEPTH, D_MODEL), f32)
    w_up = nrm(ks[9], (DEPTH, D_MODEL, D_FF), f32) * D_MODEL ** -0.5
    w_down = nrm(ks[10], (DEPTH, D_FF, D_MODEL), f32) * D_FF ** -0.5
    g_final = 1.0 + 0.02 * nrm(ks[11], (D_MODEL,), f32)
    return {"x": x, "w_in": w_in, "a_lambda": a_lambda, "a_subln": a_subln, "b_sinks": b_sinks,
            "c_fbias": c_fbias, "w_out": w_out, "g_mix": g_mix, "g_mlp": g_mlp,
            "w_up": w_up, "w_down": w_down, "g_final": g_final}

def reference(x, w_in, a_lambda, a_subln, b_sinks, c_fbias, w_out, g_mix, g_mlp, w_up, w_down, g_final):
    B, S, _ = x.shape
    slopes_a, slopes_b = alibi_slopes()
    offsets = np.cumsum(SPLIT_SIZES)[:-1].tolist()
    for l in range(DEPTH):
        h = rmsnorm(x, g_mix[l])
        proj = h @ w_in[l]
        aq, ak, av, bq, bk, bv, cq, ck, cv, cf = jnp.split(proj, offsets, axis=-1)

        lam_init = 0.8 - 0.6 * math.exp(-0.3 * l)
        lv = a_lambda[l].astype(jnp.float32)
        lam = jnp.exp(jnp.sum(lv[0] * lv[1])) - jnp.exp(jnp.sum(lv[2] * lv[3])) + lam_init
        o_a = diff_attention(aq.reshape(B, S, A_HEADS, 2, HEAD_DIM),
                             ak.reshape(B, S, A_HEADS, 2, HEAD_DIM),
                             av.reshape(B, S, A_HEADS, A_V_DIM),
                             lam, lam_init, a_subln[l], slopes_a)

        o_b = sliding_window_sink_attention(bq.reshape(B, S, B_KV_HEADS, B_GROUP, HEAD_DIM),
                                            bk.reshape(B, S, B_KV_HEADS, HEAD_DIM),
                                            bv.reshape(B, S, B_KV_HEADS, HEAD_DIM),
                                            b_sinks[l], slopes_b)

        log_f = jax.nn.log_sigmoid(cf.astype(jnp.float32) + c_fbias[l].astype(jnp.float32))
        o_c = forgetting_attention(cq.reshape(B, S, C_HEADS, HEAD_DIM),
                                   ck.reshape(B, S, C_HEADS, HEAD_DIM),
                                   cv.reshape(B, S, C_HEADS, HEAD_DIM), log_f)

        x = x + jnp.concatenate([o_a, o_b, o_c], axis=-1) @ w_out[l]
        h = rmsnorm(x, g_mlp[l])
        x = x + jnp.square(jax.nn.relu(h @ w_up[l])) @ w_down[l]
    return rmsnorm(x, g_final)


_drawn_inputs = setup_inputs


def setup_inputs(seed=0):
    import zlib

    import numpy as np

    out = dict(_drawn_inputs(seed))
    spreads = {}
    factors = {'a_subln': 4.618, 'b_sinks': 37.517, 'g_final': 23.147, 'c_fbias': 22.976, 'g_mlp': 4.792}
    for name, (base, spread) in spreads.items():
        noise = np.random.default_rng([zlib.crc32(name.encode()), seed]).standard_normal(out[name].shape)
        drawn = base * np.exp(spread * noise) if base else spread * noise
        out[name] = __import__('jax').numpy.asarray(drawn.astype(out[name].dtype))
    for name, factor in factors.items():
        out[name] = (out[name] * factor).astype(out[name].dtype)
    return out
```

```python
import math
from contextlib import ExitStack

import numpy as np

import concourse.bass as bass
from concourse import mybir

F32 = mybir.dt.float32
F32R = mybir.dt.float32r
ALU = mybir.AluOpType
ACT = mybir.ActivationFunctionType
AX = mybir.AxisListType

P = 128
BANK = 512
KB = 1024


def hybrid_encoder(nc, x, w_in, a_lambda, a_subln, b_sinks, c_fbias, w_out, g_mix, g_mlp,
                   w_up, w_down, g_final, out):
    _, S, D = x.shape
    DEPTH = w_in.shape[0]
    HD = a_lambda.shape[2]
    AH, BH, CH = 4, b_sinks.shape[1], c_fbias.shape[1]
    F = w_up.shape[2]
    CHUNK = 64
    EPS = 1e-5
    NEG = -1e30
    NC = D // P
    NQ = S // P
    GROUPS = F // D
    assert (S, D, HD, F) == (1024, 1024, 64, 4096) and NC == 8 and NQ == 8

    NPROJ = 16
    NV = 7
    NOUT = NC
    SPLIT = NPROJ + NV
    NSLAB = SPLIT + NOUT + GROUPS * 2 * NC
    OFF_AK = AH * 2 * HD
    OFF_AV = 2 * OFF_AK
    OFF_BQ = OFF_AV + AH * 2 * HD
    OFF_BK = OFF_BQ + BH * HD
    OFF_BV = OFF_BK + BH * HD // 2
    OFF_CQ = OFF_BV + BH * HD // 2
    OFF_CK = OFF_CQ + CH * HD
    OFF_CV = OFF_CK + CH * HD
    OFF_CF = OFF_CV + CH * HD
    D_IN = OFF_CF + CH
    assert D_IN == w_in.shape[2]
    Q_COLS = [P * h for h in range(AH)] + [None, None] + [OFF_CQ, OFF_CQ + P]
    K_COLS = [OFF_AK + P * h for h in range(AH)] + [OFF_BK, OFF_CK, OFF_CK + P]
    F_ROW = P - CH
    V_COLS = [OFF_AV + P * h for h in range(AH)] + [OFF_BV, OFF_CV, OFF_CV + P]
    PROJ_COLS = Q_COLS + K_COLS + [D_IN - P] + V_COLS
    PER_BUF = [(SPLIT + 1) // 2 + (NSLAB - SPLIT) // 2, SPLIT // 2 + (NSLAB - SPLIT) // 2]
    CREDIT = 2

    SLOPE_A = [2.0 ** (-8.0 * (2 * h + 1) / (AH + BH)) for h in range(AH)]
    SLOPE_B = [2.0 ** (-8.0 * (2 * h + 2) / (AH + BH)) for h in range(BH)]
    SLOPES = [(s, s) for s in SLOPE_A] + [(SLOPE_B[p], SLOPE_B[2 + p]) for p in range(2)] + [(1.0, 1.0)] * 2
    K_SLAB = [8, 9, 10, 11, 12, 12, 13, 14]
    V_SLAB = [0, 1, 2, 3, 4, 4, 5, 6]
    STEPS = 96
    MAPS = 128
    STEP0 = {"A": 0, "B": 32, "C": 64}
    MAP0 = {"A": 0, "B": 64, "C": 96}
    PAIR_END = [8, 16, 24, 32, 48, 64, 80, 96]

    x_rows = x[0].rearrange("(b p) d -> p b d", p=P)
    out_rows = out[0].rearrange("(b p) d -> p b d", p=P)
    x_saved = nc.dram_tensor("x_saved", (P, NC * S), F32, kind="Internal").ap()

    with ExitStack() as ctx:
        def sem(name):
            return ctx.enter_context(nc.semaphore(name))

        base = (nc.sbuf_base + 31) // 32 * 32

        def place(name, shape, offset, dtype=F32):
            return nc.alloc_sbuf_tensor_at(name, shape, dtype, offset=base + offset)

        W_AT, H_AT, TMP_AT, G_AT, X_AT, T_AT = 0, 24 * KB, 88 * KB, 104 * KB, 168 * KB, 200 * KB
        w_raw = place("w_raw", [P, 2, NC, P], W_AT)
        w_hi = place("w_hi", [P, 2, NC, P], W_AT + 8 * KB, F32R)
        w_lo = place("w_lo", [P, 2, NC, P], W_AT + 16 * KB, F32R)
        h_hi = place("h_hi", [P, NC, S], H_AT, F32R)
        h_lo = place("h_lo", [P, NC, S], H_AT + 32 * KB, F32R)
        q_hi = place("q_hi", [P, 2, S], H_AT, F32R)
        q_lo = place("q_lo", [P, 2, S], H_AT + 8 * KB, F32R)
        k_hi = place("k_hi", [P, 2, S], H_AT + 16 * KB, F32R)
        k_lo = place("k_lo", [P, 2, S], H_AT + 24 * KB, F32R)
        v_hi = place("v_hi", [P, 2, NQ, P], H_AT + 32 * KB, F32R)
        v_lo = place("v_lo", [P, 2, NQ, P], H_AT + 40 * KB, F32R)
        probs = place("probs", [P, 4, S], H_AT + 48 * KB)
        pt_hi = place("pt_hi", [P, 2, NQ, P], TMP_AT, F32R)
        pt_lo = place("pt_lo", [P, 2, NQ, P], TMP_AT + 8 * KB, F32R)
        ring = [place("ring0", [P, S], TMP_AT), place("ring1", [P, S], TMP_AT + 12 * KB)]
        sq_sum = place("sq_sum", [P, S], TMP_AT + 4 * KB)
        gate_tmp = place("gate_tmp", [P, S], TMP_AT + 4 * KB)
        lam_raw = place("lam_raw", [P, DEPTH * 4 * HD], TMP_AT + 4 * KB)
        inv_rms = place("inv_rms", [P, S], TMP_AT + 8 * KB)
        turn_in = [probs[:, 0], probs[:, 1]]
        raw = place("raw", [P, 16, S], G_AT)
        mix_lo = place("mix_lo", [P, NC, S], G_AT, F32R)
        mix_hi = place("mix_hi", [P, NC, S], G_AT + 32 * KB, F32R)
        u_hi = place("u_hi", [P, NC, S], G_AT, F32R)
        u_lo = place("u_lo", [P, NC, S], G_AT + 32 * KB, F32R)
        rows = place("rows", [P, NQ, D], G_AT)
        xt = place("xt", [P, NC, S], X_AT)
        v_rows = place("v_rows", [P, NQ, NV * P], X_AT)
        cursor = [T_AT]

        def small(name, shape, dtype=F32):
            t = place(name, shape, cursor[0], dtype)
            cursor[0] += (4 * int(np.prod(shape[1:])) + 31) // 32 * 32
            assert base + cursor[0] <= nc.sbuf_usable_end
            return t

        ident = small("ident", [P, P])
        ones = small("ones", [P, P])
        far = small("far", [P, S])
        near = small("near", [P, 2 * P])
        causal = small("causal", [P, P])
        NPAR = (2 * DEPTH + 1) * NC
        param = small("param", [P, 64])
        mix_gain = small("mix_gain", [P, DEPTH * NC])
        q_scale = small("q_scale", [P, NPROJ])
        slope = small("slope", [P, 16])
        neg_slope = small("neg_slope", [P, 16])
        sink_raw = small("sink_raw", [P, DEPTH * BH])
        sink = small("sink", [P, DEPTH * 4])
        neg_lam = small("neg_lam", [P, DEPTH])
        lam_dot = small("lam_dot", [P, DEPTH * 2])
        eps = small("eps", [P, 1])
        row_max = small("row_max", [P, 8])
        neg_max = small("neg_max", [P, 8])
        row_sum = small("row_sum", [P, 8])
        sink_exp = small("sink_exp", [P, 8])
        inv_sum = small("inv_sum", [P, 8])
        lam_ratio = small("lam_ratio", [P, 8])
        o_sq = small("o_sq", [P, AH * NQ])
        o_inv = small("o_inv", [P, AH * NQ])
        o_sq_now = small("o_sq_now", [P, 2 * NQ])
        slope_now = small("slope_now", [P, 4])
        wait_slot = small("wait_slot", [P, 1])
        cum_q = small("cum_q", [P, NQ * CH])
        par_raw = place("par_raw", [64, P], TMP_AT)

        ps = [ctx.enter_context(nc.psum_tensor(f"ps{i}", [P, 2 * BANK], F32)) for i in range(4)]

        w_loaded = [sem("w_loaded0"), sem("w_loaded1")]
        w_hi_done = sem("w_hi_done")
        w_split = sem("w_split")
        slab_done = sem("slab_done")
        evacuated = sem("evacuated")
        x_loaded = [sem(f"x_loaded{i}") for i in range(4)]
        x_turned = sem("x_turned")
        x_ready = sem("x_ready")
        squared = sem("squared")
        sq_added = sem("sq_added")
        h_hi_done = sem("h_hi_done")
        h_split = sem("h_split")
        ss_done = sem("ss_done")
        rms_done = sem("rms_done")
        relu_sq = sem("relu_sq")
        u_split = sem("u_split")
        vt_turned = sem("vt_turned")
        v_stored = sem("v_stored")
        x_spilled = sem("x_spilled")
        x_back = sem("x_back")
        gate_log = sem("gate_log")
        cum_ready = sem("cum_ready")
        cum_ps = sem("cum_ps")
        cum_out = sem("cum_out")
        hi_staged = sem("hi_staged")
        staged = sem("staged")
        scored = sem("scored")
        scores_read = sem("scores_read")
        max_done = sem("max_done")
        bias_done = sem("bias_done")
        exp_done = sem("exp_done")
        combined = sem("combined")
        turned = sem("turned")
        pt_hi_done = sem("pt_hi_done")
        pt_split = sem("pt_split")
        pv_done = sem("pv_done")
        o_stored = sem("o_stored")
        o_rms = sem("o_rms")
        y_ready = sem("y_ready")
        y_turned = sem("y_turned")
        mix_hi_done = sem("mix_hi_done")
        mix_split = sem("mix_split")
        setup_pool = sem("setup_pool")
        setup_dve = sem("setup_dve")
        setup_act = sem("setup_act")
        setup_pe = sem("setup_pe")
        par_loaded = sem("par_loaded")
        bc_loaded = sem("bc_loaded")
        out_done = sem("out_done")

        block = ctx.enter_context(nc.Block())

        def w_dram(matrix, l):
            return matrix[l].rearrange("(c p) n -> p c n", p=P)

        def slab_no(region, m, j):
            return 2 * m + j + (SPLIT if region else 0)

        def buf_no(region, m, j):
            return m + ((SPLIT + 1 - j) // 2 if region else 0)

        def ring_free(region, m, j):
            if region and isinstance(m, int) and m == 0:
                return SPLIT + CREDIT
            return slab_no(region, m, j) - 1 + CREDIT

        @block.sync
        def _(sp):
            for i in range(4):
                w = D // 4
                sp.dma_start(rows[:, :, i * w:(i + 1) * w], x_rows[:, :, i * w:(i + 1) * w]).then_inc(x_loaded[i], 16)
            sp.wait_ge(setup_pool, 1)
            r = 0
            for l in range(DEPTH):
                for g in (g_mix, g_mlp):
                    sp.dma_start(par_raw[r:r + NC, :], g[l].rearrange("(c p) -> c p", p=P)).then_inc(par_loaded, 16)
                    r += NC
            sp.dma_start(par_raw[r:r + NC, :], g_final.rearrange("(c p) -> c p", p=P)).then_inc(par_loaded, 16)
            sp.dma_start(par_raw[NPAR:NPAR + DEPTH, :], a_subln).then_inc(par_loaded, 16)
            sp.dma_start(par_raw[NPAR + DEPTH:NPAR + 2 * DEPTH, F_ROW:P], c_fbias).then_inc(par_loaded, 16)
            sp.dma_start(lam_raw[:], a_lambda.rearrange("(o l) k d -> o (l k d)", o=1).to_broadcast([P, DEPTH * 4 * HD])).then_inc(bc_loaded, 16)
            sp.dma_start(sink_raw[:], b_sinks.rearrange("(o l) h -> o (l h)", o=1).to_broadcast([P, DEPTH * BH])).then_inc(bc_loaded, 16)

            def load(l, region, m, j, parts):
                sp.wait_ge(w_split, NSLAB * l + ring_free(region, m, j))
                for dst, src in parts:
                    sp.dma_start(dst, src).then_inc(w_loaded[j], 16)

            def halves(j, src):
                h = NC // 2
                return [(w_raw[:, j, 0:h], src[:, 0:h]), (w_raw[:, j, h:NC], src[:, h:NC])]

            with sp.Fori(0, DEPTH) as l:
                win = w_dram(w_in, l)

                def load_proj(s):
                    c0 = PROJ_COLS[s]
                    if c0 is None:
                        at = OFF_BQ + HD * (s - 4)
                        parts = [(w_raw[:, s % 2, :, g * HD:(g + 1) * HD],
                                  win[:, :, at + 2 * HD * g:at + 2 * HD * g + HD]) for g in range(2)]
                    else:
                        parts = halves(s % 2, win[:, :, c0:c0 + P])
                    load(l, 0, s // 2, s % 2, parts)

                for s in range(2):
                    load_proj(s)
                sp.wait_ge(h_split, 2 * NC * l + NC)
                sp.dma_start(x_saved, xt[:].rearrange("p c s -> p (c s)")).then_inc(x_spilled, 16)
                for s in range(2, SPLIT):
                    load_proj(s)
                wo = w_dram(w_out, l).rearrange("p c (m j n) -> m j p c n", j=2, n=P)
                for j in range(2):
                    load(l, 1, 0, j, halves(j, wo[0, j]))
                sp.wait_ge(pv_done, STEPS * l + STEPS)
                sp.dma_start(xt[:].rearrange("p c s -> p (c s)"), x_saved).then_inc(x_back, 16)
                with sp.Fori(1, NOUT // 2) as m:
                    for j in range(2):
                        load(l, 1, m, j, halves(j, wo[m, j]))
                up = w_dram(w_up, l).rearrange("p c (g m j n) -> g m j p c n", g=GROUPS, j=2, n=P)
                down = w_down[l].rearrange("(g c p) (m j n) -> g m j p c n", p=P, c=NC, j=2, n=P)
                with sp.Fori(0, GROUPS) as g:
                    with sp.Fori(0, NC // 2) as m:
                        for j in range(2):
                            load(l, 1, NC * g + (m + NC // 2), j, halves(j, up[g, m, j]))
                    with sp.Fori(0, NC // 2) as m:
                        for j in range(2):
                            load(l, 1, NC * g + (m + NC), j, halves(j, down[g, m, j]))
            for i in range(4):
                w = D // 4
                sp.wait_ge(mix_hi_done, NC * DEPTH + 2 * (i + 1))
                sp.dma_start(out_rows[:, :, i * w:(i + 1) * w], rows[:, :, i * w:(i + 1) * w]).then_inc(out_done, 16)
            sp.wait_ge(out_done, 4 * 16)

        @block.gpsimd
        def _(pool):
            pool.memset(par_raw[:], 0.0).then_inc(setup_pool, 1)
            pool.memset(ident[:], 0.0).then_inc(setup_pool, 1)
            pool.memset(causal[:], 0.0).then_inc(setup_pool, 1)
            pool.iota(far[:], [[-1, S]], base=S - P, channel_multiplier=1,
                      allow_small_or_imprecise_dtypes=True).then_inc(setup_pool, 1)
            pool.iota(near[:], [[-1, 2 * P]], base=P, channel_multiplier=1,
                      allow_small_or_imprecise_dtypes=True).then_inc(setup_pool, 1)
            pool.wait_ge(setup_pool, 5)
            pool.affine_select(out=ident[:], in_=ident[:], compare_op=ALU.not_equal, fill=1.0, base=0,
                               pattern=[[-1, P]], channel_multiplier=1).then_inc(setup_pool, 1)
            pool.affine_select(out=causal[:], in_=causal[:], compare_op=ALU.is_ge, fill=NEG, base=0,
                               pattern=[[-1, P]], channel_multiplier=1).then_inc(setup_pool, 1)
            def add_squares(n0, c, slot):
                pool.wait_ge(squared, n0 + (c + 1))
                if isinstance(c, int) and c == 0:
                    nc.gpsimd.tensor_tensor(sq_sum[:], ring[slot][:], ones[:, 0:1].to_broadcast([P, S]),
                                            ALU.mult).then_inc(sq_added, 1)
                else:
                    pool.wait_ge(sq_added, n0 + (c + CREDIT))
                    nc.gpsimd.tensor_tensor(sq_sum[:], sq_sum[:], ring[slot][:], ALU.add).then_inc(sq_added, 1)

            def norm_squares(n0):
                for c in range(NC):
                    add_squares(n0, c, c % 2)

            pool.sem_inc(sq_added, CREDIT)
            norm_squares(0)
            with pool.Fori(0, DEPTH) as l:
                def stage_lo(n, q, k, v, pp):
                    pool.wait_ge(hi_staged, 8 * l + (n + 1))
                    for lo, hi, src in ((q_lo[:, pp], q_hi[:, pp], raw[:, q]), (k_lo[:, pp], k_hi[:, pp], raw[:, k]),
                                        (v_lo[:, pp], v_hi[:, pp], v_rows[:, :, bass.ts(v, P)])):
                        nc.gpsimd.tensor_tensor(lo, src, hi.bitcast(F32), ALU.subtract).then_inc(staged, 1)

                with pool.Fori(0, 2) as a:
                    for pp in range(2):
                        stage_lo(2 * a + pp, 2 * a + pp, 2 * a + (8 + pp), 2 * a + pp, pp)
                for n in range(4, 8):
                    stage_lo(n, n, K_SLAB[n], V_SLAB[n], n % 2)
                norm_squares(2 * NC * l + NC)
                norm_squares(2 * NC * l + 2 * NC)

        @block.scalar
        def _(act):
            def split_w(l, region, m, j):
                act.wait_ge(w_loaded[j], 32 * PER_BUF[j] * l + 32 * buf_no(region, m, j) + 32)
                act.wait_ge(slab_done, NSLAB * l + ring_free(region, m, j))
                nc.scalar.activation(w_hi[:, j], w_raw[:, j], ACT.Copy).then_inc(w_hi_done, 1)

            def prepare(n0, gain, c, slot):
                act.wait_ge(sq_added, n0 + c + 1)
                nc.scalar.activation(ring[slot][:], xt[:, c], ACT.Square).then_inc(squared, 1)
                nc.scalar.activation(h_hi[:, c], xt[:, c], ACT.Copy,
                                     scale=param[:, bass.ds(gain, 1)]).then_inc(h_hi_done, 1)

            def root_mean_square(n):
                act.wait_ge(ss_done, n)
                nc.scalar.activation(inv_rms[:], ps[2][:], ACT.Sqrt, bias=eps[:, 0:1], scale=1.0 / D).then_inc(rms_done, 1)

            act.sem_inc(o_stored, CREDIT)
            act.wait_ge(setup_dve, 1)
            nc.scalar.activation(lam_dot[:], lam_dot[:], ACT.Exp).then_inc(setup_act, 1)
            for c in range(NC):
                act.wait_ge(x_ready, c + 1)
                prepare(0, c, c, c % 2)

            with act.Fori(0, DEPTH) as l:
                split_w(l, 0, 0, 0)
                split_w(l, 0, 0, 1)
                root_mean_square(2 * l + 1)
                with act.Fori(1, NPROJ // 2) as m:
                    for j in range(2):
                        split_w(l, 0, m, j)
                split_w(l, 0, NPROJ // 2, 0)
                act.wait_ge(evacuated, NSLAB * l + NPROJ + CREDIT)
                g_in, g_tmp = raw[96:P, 15], gate_tmp[96:P]
                bias = param[96:P, bass.ds(l + (NPAR + DEPTH), 1)]
                nc.scalar.activation(g_tmp, g_in, ACT.Abs, bias=bias)
                act.drain()
                nc.scalar.activation(g_tmp, g_tmp, ACT.Exp, scale=-1.0)
                act.drain()
                nc.scalar.activation(g_tmp, g_tmp, ACT.Ln, bias=1.0).then_inc(gate_log, 1)

                def store_v(v, slot):
                    act.wait_ge(vt_turned, NV * l + v + (1 + CREDIT))
                    nc.scalar.activation(v_rows[:, :, bass.ts(v, P)], ps[2 + slot][:].rearrange("p (b d) -> p b d", d=P),
                                         ACT.Copy).then_inc(v_stored, 1)

                split_w(l, 0, 8, 1)
                act.wait_ge(x_spilled, 16 * l + 16)
                store_v(0, 0)
                for v in range(1, NV):
                    if v < NV - 1:
                        split_w(l, 0, (NPROJ + v + 1) // 2, (v + 1) % 2)
                    else:
                        split_w(l, 1, 0, 0)
                    store_v(v, v % 2)
                act.drain()

                def stage_hi(n, q, k, v, pp, ended):
                    if ended is not None:
                        act.wait_ge(pv_done, ended)
                    nc.scalar.activation(q_hi[:, pp], raw[:, q], ACT.Copy)
                    nc.scalar.activation(k_hi[:, pp], raw[:, k], ACT.Copy)
                    nc.scalar.activation(v_hi[:, pp], v_rows[:, :, bass.ts(v, P)], ACT.Copy).then_inc(hi_staged, 1)

                def forget_bias(grp, t):
                    pp, i, j = t // 16, (t // 2) % NQ, t % 2
                    act.wait_ge(turned, STEPS * l + STEP0["C"] + t - 1)
                    if i:
                        nc.scalar.activation(probs[:, t % 4, 0:i * P], raw[:, 8 + 2 * pp + j, 0:i * P], ACT.Identity,
                                             bias=cum_q[:, i * CH + 2 * pp + j:i * CH + 2 * pp + j + 1])\
                            .then_inc(bias_done, 1)

                def probs_hi(s0, t, width):
                    act.wait_ge(turned, s0 + (t + 1 + CREDIT))
                    nc.scalar.activation(pt_hi[:, t % 2].rearrange("p b q -> p (b q)")[:, 0:width],
                                         ps[2][:, 0:width], ACT.Copy).then_inc(pt_hi_done, 1)

                def store_o(s0, t, slab, i, j, n, square):
                    act.wait_ge(pv_done, s0 + (t + 1))
                    act.wait_ge(combined, s0 + (t + 1))
                    w = P if square is not None else HD
                    at = i * P + (0 if square is not None else HD * j)
                    o = ps[3][:, BANK * (t % 2):BANK * (t % 2) + w]
                    inv = inv_sum[:, n % 8:n % 8 + 1]
                    if square is not None:
                        nc.scalar.activation(ps[3][:, BANK * (t % 2) + P:BANK * (t % 2) + 2 * P], o, ACT.Square, scale=inv,
                                             accum_out=o_sq_now[:, square:square + 1])
                    store = nc.scalar.activation(raw[:, slab, at:at + w], o, ACT.Copy, scale=inv)
                    store.then_inc(o_stored, 1)

                def exponentials(m0, n, width, sl, sink_at=None):
                    act.wait_ge(max_done, m0 + (n + 1))
                    e = nc.scalar.activation(probs[:, n % 4, 0:width], probs[:, n % 4, 0:width], ACT.Exp,
                                             bias=neg_max[:, n % 8:n % 8 + 1], scale=sl,
                                             accum_out=row_sum[:, n % 8:n % 8 + 1])
                    if sink_at is not None:
                        e = nc.scalar.activation(sink_exp[:, n % 8:n % 8 + 1], sink[:, bass.ds(sink_at, 1)], ACT.Exp,
                                                 bias=neg_max[:, n % 8:n % 8 + 1], scale=sl)
                    e.then_inc(exp_done, 1)

                act.wait_ge(slab_done, NSLAB * l + SPLIT + CREDIT)
                stage_hi(0, 0, 8, 0, 0, None)

                with act.Fori(0, 2) as a:
                    s0, m0 = STEPS * l + 16 * a, MAPS * l + 32 * a
                    nc.scalar.activation(slope_now[:], slope[:, bass.ds(4 * a, 4)], ACT.Copy)
                    act.drain()
                    for t in range(16 + 2):
                        if t >= 2:
                            probs_hi(s0, t - 2, ((t - 2) % NQ + 1) * P)
                        if t < 16:
                            pp, i = t // NQ, t % NQ
                            for j in range(2):
                                exponentials(m0, 2 * t + j, (i + 1) * P, slope_now[:, 2 * pp + j:2 * pp + j + 1])
                        if t >= 2:
                            pp, i = (t - 2) // NQ, (t - 2) % NQ
                            store_o(s0, t - 2, 2 * a + pp, i, 0, 2 * (t - 2), t - 2)
                        if t % NQ == 3 and t < 16:
                            pp = t // NQ
                            n = 2 * a + (pp + 1)
                            if pp == 0:
                                stage_hi(n, n, 2 * a + 9, n, 1, None)
                            else:
                                stage_hi(n, n, 2 * a + 10, n, 0, s0 + 8)

                    act.drain()
                    nc.scalar.activation(o_sq[:, bass.ts(a, 2 * NQ)], o_sq_now[:], ACT.Copy)

                for h in range(CH):
                    act.wait_ge(cum_ps, 5 * l + h + 1)
                    nc.scalar.activation(raw[:, 8 + h], ps[h % 2][:], ACT.Copy, scale=-1.0).then_inc(cum_out, 1)
                act.wait_ge(cum_ps, 5 * l + 5)
                nc.scalar.activation(cum_q[:].rearrange("p (b h) -> p b h", h=CH),
                                     ps[2][:, 0:NQ * 32].rearrange("p (b h) -> p b h", h=32)[:, :, 32 - CH:32],
                                     ACT.Copy).then_inc(cum_out, 1)
                act.drain()

                for grp in "BC":
                    s0, m0 = STEPS * l + STEP0[grp], MAPS * l + MAP0[grp]
                    q0 = 4 if grp == "B" else 6
                    if grp == "C":
                        forget_bias(grp, 0)
                    for t in range(32 + 2):
                        if t >= 2:
                            i = ((t - 2) // 2) % NQ
                            probs_hi(s0, t - 2, (i + 1) * P if grp == "C" else min(i + 1, 2) * P)
                        if grp == "C" and t + 1 < 32:
                            forget_bias(grp, t + 1)
                        if t < 32:
                            pp, i, j = t // 16, (t // 2) % NQ, t % 2
                            width = (i + 1) * P if grp == "C" else min(i + 1, 2) * P
                            at = 2 * (q0 + pp) + j
                            exponentials(m0, t, width, slope[:, at:at + 1],
                                         4 * l + (2 * pp + j) if grp == "B" else None)
                        if t >= 2:
                            u = t - 2
                            store_o(s0, u, q0 + u // 16, (u // 2) % NQ, u % 2, u, None)
                        if t in (5, 21) and (grp, t) != ("C", 21):
                            n = q0 + t // 16 + 1
                            stage_hi(n, n, K_SLAB[n], V_SLAB[n], n % 2, STEPS * l + PAIR_END[n - 2])

                act.drain()
                nc.scalar.activation(o_inv[:], o_sq[:], ACT.Sqrt, bias=eps[:, 0:1], scale=1.0 / P).then_inc(o_rms, 1)
                with act.Fori(0, NC // 2) as m:
                    for j in range(2):
                        act.wait_ge(y_turned, NC * l + 2 * m + (j + 1))
                        nc.scalar.activation(mix_hi[:, 2 * m + j], ps[j][:], ACT.Copy,
                                             scale=mix_gain[:, bass.ds(NC * l + 2 * m + j, 1)]).then_inc(mix_hi_done, 1)

                def prepared(n0, gain, m_slab, m, j, n_slab):
                    act.wait_ge(evacuated, NSLAB * l + n_slab + (1 + CREDIT))
                    prepare(n0, gain, 2 * m + j, j)

                with act.Fori(0, NOUT // 2) as m:
                    for j in range(2):
                        split_w(l, 1, m + j, 1 - j)
                        prepared(2 * NC * l + NC, 2 * NC * l + NC + 2 * m + j, m, m, j, slab_no(1, m, j))

                def hidden(g, m, j):
                    act.wait_ge(evacuated, NSLAB * l + slab_no(1, NC * g + m + NC // 2, j) + (1 + CREDIT))
                    nc.scalar.activation(ring[j][:], ring[j][:], ACT.Square)
                    act.drain()
                    nc.scalar.activation(u_hi[:, 2 * m + j], ring[j][:], ACT.Copy).then_inc(relu_sq, 1)

                split_w(l, 1, NC // 2, 1)
                root_mean_square(2 * l + 2)
                hidden(0, 0, 0)
                split_w(l, 1, NC // 2 + 1, 0)
                hidden(0, 0, 1)

                def up(g, m):
                    for j in range(2):
                        split_w(l, 1, NC * g + m + (NC // 2 + j), 1 - j)
                        hidden(g, m, j)

                def down(g, m, last):
                    for j in range(2):
                        if not (last and isinstance(m, int) and j == 1):
                            split_w(l, 1, NC * g + m + (NC + j), 1 - j)
                        if last:
                            prepared(2 * NC * l + 2 * NC, 2 * NC * l + 2 * NC + 2 * m + j, m, m, j,
                                     slab_no(1, NC * g + m + NC, j))

                with act.Fori(1, NC // 2) as m:
                    up(0, m)
                with act.Fori(0, NC // 2) as m:
                    down(0, m, False)
                with act.Fori(1, GROUPS - 1) as g:
                    with act.Fori(0, NC // 2) as m:
                        up(g, m)
                    with act.Fori(0, NC // 2) as m:
                        down(g, m, False)
                with act.Fori(0, NC // 2) as m:
                    up(GROUPS - 1, m)
                with act.Fori(0, NC // 2 - 1) as m:
                    down(GROUPS - 1, m, True)
                down(GROUPS - 1, NC // 2 - 1, True)

            root_mean_square(2 * DEPTH + 1)
            for c in range(NC):
                act.wait_ge(y_turned, NC * DEPTH + c + 1)
                nc.scalar.activation(rows[:, :, c * P:(c + 1) * P], ps[c % 2][:].rearrange("p (b d) -> p b d", d=P),
                                     ACT.Copy).then_inc(mix_hi_done, 1)

        @block.vector
        def _(dve):
            V = nc.vector

            V.memset(ones[:], 1.0)
            V.memset(eps[:], EPS)
            for q, (s_lo, s_hi) in enumerate(SLOPES):
                for j, s in enumerate((s_lo, s_hi)):
                    V.memset(slope[:, 2 * q + j:2 * q + j + 1], s)
                    V.memset(neg_slope[:, 2 * q + j:2 * q + j + 1], -s)
                    V.memset(q_scale[j * HD:(j + 1) * HD, q:q + 1], HD ** -0.5 / s)
            V.memset(q_scale[:, 8:NPROJ], 1.0)
            V.memset(mix_gain[:], 1.0)
            dve.wait_ge(setup_pool, 5)
            for t in (far, near):
                V.scalar_tensor_tensor(out=t[:], in0=t[:], scalar=-1.0, in1=t[:], op0=ALU.mult, op1=ALU.min)
            V.drain()
            for t, w in ((far, S), (near, 2 * P)):
                V.memset(t[0:CHUNK, w - CHUNK:w], NEG)
            V.memset(near[:, 0:CHUNK], NEG)
            V.memset(near[CHUNK:P, CHUNK:P], NEG)
            dve.wait_ge(bc_loaded, 32)
            lam4 = lam_raw[:].rearrange("p (a k d) -> p a k d", k=2, d=HD)
            lam_prod = ring[1][:, 0:DEPTH * 2 * HD].rearrange("p (a d) -> p a d", d=HD)
            V.tensor_tensor(lam_prod, lam4[:, :, 0], lam4[:, :, 1], ALU.mult)
            V.drain()
            V.tensor_reduce(lam_dot[:], lam_prod, AX.X, ALU.add).then_inc(setup_dve, 1)
            for l in range(DEPTH):
                for p in range(2):
                    for j in range(2):
                        at = 4 * l + 2 * p + j
                        h = 2 * j + p
                        V.tensor_scalar(sink[:, at:at + 1], sink_raw[:, l * BH + h:l * BH + h + 1], 1.0 / SLOPE_B[h],
                                        None, ALU.mult)
            dve.wait_ge(setup_act, 1)
            for l in range(DEPTH):
                lam_init = 0.8 - 0.6 * math.exp(-0.3 * l)
                V.tensor_tensor(neg_lam[:, l:l + 1], lam_dot[:, 2 * l + 1:2 * l + 2], lam_dot[:, 2 * l:2 * l + 1],
                                ALU.subtract)
                V.drain()
                V.tensor_scalar(neg_lam[:, l:l + 1], neg_lam[:, l:l + 1], -lam_init, None, ALU.add)
            dve.wait_ge(setup_pe, 1)
            V.tensor_copy(param[:], ps[3][:, 0:64])
            V.drain()
            for l in range(DEPTH):
                lam_init = 0.8 - 0.6 * math.exp(-0.3 * l)
                for c in range(AH):
                    V.tensor_scalar(mix_gain[:, l * NC + c:l * NC + c + 1], param[:, NPAR + l:NPAR + l + 1],
                                    1.0 - lam_init, None, ALU.mult)
            V.drain()
            dve.sem_inc(w_split, CREDIT)
            dve.sem_inc(evacuated, CREDIT)
            dve.sem_inc(scores_read, CREDIT)
            dve.sem_inc(pt_split, 1)
            dve.sem_inc(mix_split, CREDIT)

            def split_w(l, region, m, j):
                dve.wait_ge(w_hi_done, NSLAB * l + slab_no(region, m, j) + 1)
                V.tensor_tensor(w_lo[:, j], w_raw[:, j], w_hi[:, j].bitcast(F32), ALU.subtract).then_inc(w_split, 1)

            def result(l, region, m, j):
                dve.wait_ge(slab_done, NSLAB * l + slab_no(region, m, j) + (1 + CREDIT))
                return ps[j][:]

            def h_low(n0, gain, c):
                dve.wait_ge(h_hi_done, n0 + c + 1)
                V.scalar_tensor_tensor(out=h_lo[:, c], in0=xt[:, c], scalar=param[:, bass.ds(gain, 1)],
                                       in1=h_hi[:, c].bitcast(F32), op0=ALU.mult, op1=ALU.subtract).then_inc(h_split, 1)

            def invert_rms(n):
                dve.wait_ge(rms_done, n)
                V.reciprocal(inv_rms[:], inv_rms[:])
                V.drain()

            for c in range(NC):
                dve.wait_ge(x_turned, c + 1)
                V.tensor_copy(xt[:, c], ps[c % 2][:]).then_inc(x_ready, 1)
                if c:
                    h_low(0, c - 1, c - 1)
            h_low(0, NC - 1, NC - 1)

            with dve.Fori(0, DEPTH) as l:
                def project(s, m, j):
                    r = result(l, 0, m, j)
                    V.scalar_tensor_tensor(out=raw[:, s], in0=r, scalar=q_scale[:, bass.ds(s, 1)], in1=inv_rms[:],
                                           op0=ALU.mult, op1=ALU.mult).then_inc(evacuated, 1)

                split_w(l, 0, 0, 0)
                split_w(l, 0, 0, 1)
                invert_rms(2 * l + 1)
                project(0, 0, 0)
                split_w(l, 0, 1, 0)
                project(1, 0, 1)
                with dve.Fori(1, NPROJ // 2) as m:
                    for j in range(2):
                        split_w(l, 0, m + j, 1 - j)
                        project(2 * m + j, m, j)

                def value(v, m, j):
                    r = result(l, 0, m, j)
                    dve.wait_ge(vt_turned, NV * l + v - 1 + CREDIT)
                    V.tensor_tensor(ring[j][:], r, inv_rms[:], ALU.mult).then_inc(evacuated, 1)

                split_w(l, 0, 8, 1)
                value(0, 8, 0)
                dve.wait_ge(gate_log, l + 1)
                g_in, g_tmp = raw[96:P, 15], gate_tmp[96:P]
                V.tensor_scalar(g_in, g_in, param[96:P, bass.ds(l + (NPAR + DEPTH), 1)], 0.0, ALU.add, ALU.min)
                V.drain()
                V.tensor_tensor(g_tmp, g_in, g_tmp, ALU.subtract)
                V.drain()
                V.tensor_tensor_scan(g_in, ones[96:P, 0:1].to_broadcast([32, S]), g_tmp, 0.0, ALU.mult, ALU.add)\
                    .then_inc(cum_ready, 1)
                for v in range(1, NV):
                    s = NPROJ + v
                    if v < NV - 1:
                        split_w(l, 0, (s + 1) // 2, (s + 1) % 2)
                    value(v, s // 2, s % 2)
                split_w(l, 1, 0, 0)

                def probs_lo(s0, t, width):
                    dve.wait_ge(pt_hi_done, s0 + (t + 1))
                    flat = slice(0, width)
                    V.tensor_tensor(pt_lo[:, t % 2].rearrange("p b q -> p (b q)")[:, flat], ps[2][:, flat],
                                    pt_hi[:, t % 2].rearrange("p b q -> p (b q)")[:, flat].bitcast(F32),
                                    ALU.subtract).then_inc(pt_split, 1)

                def biased_max(s0, m0, t, n, width, bias, sc, sink_at=None):
                    dve.wait_ge(scored, m0 + (n + 1))
                    dve.wait_ge(turned, s0 + (t - 1 + CREDIT))
                    V.memset(wait_slot[:], 0.0)
                    at = n % 8
                    V.tensor_tensor_reduce(out=probs[:, n % 4, 0:width], in0=ps[n % 2][:, 0:width], in1=bias, scale=1.0,
                                           scalar=-3e38, op0=ALU.add, op1=ALU.max, accum_out=row_max[:, at:at + 1])\
                        .then_inc(scores_read, 1)
                    V.drain()
                    neg = neg_slope[:, bass.ds(sc, 1)]
                    if sink_at is None:
                        e = V.tensor_scalar(neg_max[:, at:at + 1], row_max[:, at:at + 1], neg, None, ALU.mult)
                    else:
                        e = V.tensor_scalar(neg_max[:, at:at + 1], row_max[:, at:at + 1],
                                            sink[:, bass.ds(sink_at, 1)], neg, ALU.max, ALU.mult)
                    e.then_inc(max_done, 1)

                def combine(s0, m0, t):
                    dve.wait_ge(exp_done, m0 + (2 * t + 2))
                    c, s, width = (2 * t) % 8, (2 * t) % 4, (t % NQ + 1) * P
                    V.reciprocal(inv_sum[:, c:c + 2], row_sum[:, c:c + 2])
                    V.drain()
                    V.tensor_scalar(lam_ratio[:, c:c + 1], inv_sum[:, c + 1:c + 2], row_sum[:, c:c + 1],
                                    neg_lam[:, bass.ds(l, 1)], ALU.mult, ALU.mult)
                    V.drain()
                    V.scalar_tensor_tensor(out=probs[:, s, 0:width], in0=probs[:, s + 1, 0:width],
                                           scalar=lam_ratio[:, c:c + 1], in1=probs[:, s, 0:width],
                                           op0=ALU.mult, op1=ALU.add).then_inc(combined, 1)

                def invert_sum(m0, t, with_sink):
                    dve.wait_ge(exp_done, m0 + (t + 1))
                    c = t % 8
                    if with_sink:
                        V.tensor_tensor(row_sum[:, c:c + 1], row_sum[:, c:c + 1], sink_exp[:, c:c + 1], ALU.add)
                        V.drain()
                    V.reciprocal(inv_sum[:, c:c + 1], row_sum[:, c:c + 1]).then_inc(combined, 1)

                with dve.Fori(0, 2) as a:
                    s0, m0 = STEPS * l + 16 * a, MAPS * l + 32 * a
                    for t in range(16 + 2):
                        if t >= 2:
                            probs_lo(s0, t - 2, ((t - 2) % NQ + 1) * P)
                        if 1 <= t < 17:
                            combine(s0, m0, t - 1)
                        if t < 16:
                            pp, i = t // NQ, t % NQ
                            for j in range(2):
                                biased_max(s0, m0, t, 2 * t + j, (i + 1) * P, far[:, S - (i + 1) * P:S],
                                           4 * a + (2 * pp + j))
                dve.wait_ge(cum_out, 5 * l + 5)
                for grp in "BC":
                    s0, m0 = STEPS * l + STEP0[grp], MAPS * l + MAP0[grp]
                    q0 = 4 if grp == "B" else 6
                    for t in range(32 + 2):
                        if t >= 2:
                            i = ((t - 2) // 2) % NQ
                            probs_lo(s0, t - 2, (i + 1) * P if grp == "C" else min(i + 1, 2) * P)
                        if 1 <= t < 33:
                            invert_sum(m0, t - 1, grp == "B")
                        if t < 32:
                            pp, i, j = t // 16, (t // 2) % NQ, t % 2
                            if grp == "B":
                                width = min(i + 1, 2) * P
                                biased_max(s0, m0, t, t, width, near[:, 2 * P - width:2 * P], 2 * (q0 + pp) + j,
                                           4 * l + (2 * pp + j))
                            else:
                                width = (i + 1) * P
                                h = 2 * pp + j
                                if i:
                                    dve.wait_ge(bias_done, 28 * l + 14 * pp + 2 * (i - 1) + j + 1)
                                V.scalar_tensor_tensor(out=probs[:, t % 4, i * P:width], in0=raw[:, 8 + h, i * P:width],
                                                       scalar=cum_q[:, i * CH + h:i * CH + h + 1], in1=causal[:],
                                                       op0=ALU.add, op1=ALU.add)
                                V.drain()
                                biased_max(s0, m0, t, t, width, probs[:, t % 4, 0:width], 2 * (q0 + pp) + j)

                dve.wait_ge(o_rms, l + 1)
                V.reciprocal(o_inv[:], o_inv[:])
                V.drain()
                o_all = raw[:].rearrange("p s (b e) -> p s b e", e=P)
                for c in range(NC + 1):
                    if c < NC:
                        dve.wait_ge(y_turned, NC * l + c - 1) if c >= 2 else None
                        y = turn_in[c % 2].rearrange("p (b e) -> p b e", e=P)
                        if c < AH:
                            V.tensor_tensor(y, o_all[:, c], o_inv[:, c * NQ:(c + 1) * NQ].unsqueeze(2).to_broadcast([P, NQ, P]),
                                            ALU.mult).then_inc(y_ready, 1)
                        elif c < AH + 2:
                            g = c - AH
                            yb = turn_in[c % 2].rearrange("p (b s e) -> p s b e", s=2, e=HD)
                            for s in range(2):
                                e = V.tensor_copy(yb[:, s], o_all[:, 4 + s, :, g * HD:(g + 1) * HD])
                            e.then_inc(y_ready, 1)
                            V.drain()
                        else:
                            V.tensor_copy(y, o_all[:, c]).then_inc(y_ready, 1)
                    if c:
                        dve.wait_ge(mix_hi_done, NC * l + c)
                        V.scalar_tensor_tensor(out=mix_lo[:, c - 1], in0=ps[(c - 1) % 2][:],
                                               scalar=mix_gain[:, bass.ds(NC * l + (c - 1), 1)],
                                               in1=mix_hi[:, c - 1].bitcast(F32), op0=ALU.mult,
                                               op1=ALU.subtract).then_inc(mix_split, 1)

                def residual(mm, m, j):
                    r = result(l, 1, mm, j)
                    V.tensor_tensor(xt[:, 2 * m + j], r, xt[:, 2 * m + j], ALU.add).then_inc(evacuated, 1)

                with dve.Fori(0, NOUT // 2) as m:
                    for j in range(2):
                        split_w(l, 1, m + j, 1 - j)
                        dve.wait_ge(x_back, 16 * l + 16)
                        residual(m, m, j)
                        dve.wait_ge(h_hi_done, 2 * NC * l + 2 * m + (NC + j + 1))
                        V.scalar_tensor_tensor(out=h_lo[:, 2 * m + j], in0=xt[:, 2 * m + j],
                                               scalar=param[:, bass.ds(2 * NC * l + 2 * m + (NC + j), 1)],
                                               in1=h_hi[:, 2 * m + j].bitcast(F32), op0=ALU.mult,
                                               op1=ALU.subtract).then_inc(h_split, 1)

                def hidden(g, m, j):
                    r = result(l, 1, NC * g + m + NC // 2, j)
                    V.scalar_tensor_tensor(out=ring[j][:], in0=r, scalar=0.0, in1=inv_rms[:], op0=ALU.max,
                                           op1=ALU.mult).then_inc(evacuated, 1)
                    dve.wait_ge(relu_sq, 4 * NC * l + NC * g + 2 * m + (j + 1))
                    V.tensor_tensor(u_lo[:, 2 * m + j], ring[j][:], u_hi[:, 2 * m + j].bitcast(F32),
                                    ALU.subtract).then_inc(u_split, 1)

                split_w(l, 1, NC // 2, 1)
                invert_rms(2 * l + 2)
                hidden(0, 0, 0)
                split_w(l, 1, NC // 2 + 1, 0)
                hidden(0, 0, 1)

                def up(g, m):
                    for j in range(2):
                        split_w(l, 1, NC * g + m + (NC // 2 + j), 1 - j)
                        hidden(g, m, j)

                def down(g, m, last):
                    for j in range(2):
                        if not (last and isinstance(m, int) and j == 1):
                            split_w(l, 1, NC * g + m + (NC + j), 1 - j)
                        residual(NC * g + m + NC, m, j)
                        if last:
                            dve.wait_ge(h_hi_done, 2 * NC * l + 2 * m + (2 * NC + j + 1))
                            V.scalar_tensor_tensor(out=h_lo[:, 2 * m + j], in0=xt[:, 2 * m + j],
                                                   scalar=param[:, bass.ds(2 * NC * l + 2 * m + (2 * NC + j), 1)],
                                                   in1=h_hi[:, 2 * m + j].bitcast(F32), op0=ALU.mult,
                                                   op1=ALU.subtract).then_inc(h_split, 1)

                with dve.Fori(1, NC // 2) as m:
                    up(0, m)
                with dve.Fori(0, NC // 2) as m:
                    down(0, m, False)
                with dve.Fori(1, GROUPS - 1) as g:
                    with dve.Fori(0, NC // 2) as m:
                        up(g, m)
                    with dve.Fori(0, NC // 2) as m:
                        down(g, m, False)
                with dve.Fori(0, NC // 2) as m:
                    up(GROUPS - 1, m)
                with dve.Fori(0, NC // 2 - 1) as m:
                    down(GROUPS - 1, m, True)
                down(GROUPS - 1, NC // 2 - 1, True)

            invert_rms(2 * DEPTH + 1)
            for c in range(NC):
                if c >= 2:
                    dve.wait_ge(y_turned, NC * DEPTH + c - 1)
                V.scalar_tensor_tensor(out=turn_in[c % 2], in0=xt[:, c],
                                       scalar=param[:, 2 * DEPTH * NC + c:2 * DEPTH * NC + c + 1], in1=inv_rms[:],
                                       op0=ALU.mult, op1=ALU.mult).then_inc(y_ready, 1)

        @block.tensor
        def _(pe):
            def products(region, m, j, l, hi, lo, ready, count):
                pe.wait_ge(w_split, NSLAB * l + slab_no(region, m, j) + (1 + CREDIT))
                pe.wait_ge(evacuated, NSLAB * l + ring_free(region, m, j))
                pe.wait_ge(ready, count - 1)
                for c in range(NC):
                    if c == NC - 1:
                        pe.wait_ge(ready, count)
                    for n, (w, h) in enumerate(((w_hi, hi), (w_hi, lo), (w_lo, hi))):
                        for t in range(S // BANK):
                            mm = nc.tensor.matmul(ps[j][:, bass.ts(t, BANK)], w[:, j, c], h[:, c, bass.ts(t, BANK)],
                                                  start=(c == 0 and n == 0), stop=(c == NC - 1 and n == 2))
                mm.then_inc(slab_done, 1)

            def turn(src, dst, count, done, size=P, idn=None):
                for b in range(count):
                    tr = nc.tensor.transpose(dst[:, b * P:(b + 1) * P], src[:, b * P:(b + 1) * P], ident[:])
                tr.then_inc(done, 1)

            def sum_squares(n):
                pe.wait_ge(sq_added, NC * n + CREDIT)
                for t in range(S // BANK):
                    mm = nc.tensor.matmul(ps[2][:, bass.ts(t, BANK)], ones[:], sq_sum[:, bass.ts(t, BANK)],
                                          start=True, stop=True)
                mm.then_inc(ss_done, 1)

            pe.sem_inc(slab_done, CREDIT)
            pe.sem_inc(vt_turned, CREDIT)
            pe.sem_inc(turned, CREDIT)
            pe.wait_ge(setup_pool, 6)
            pe.wait_ge(par_loaded, 16 * (2 * DEPTH + 3))
            nc.tensor.transpose(ps[3][:, 0:64], par_raw[:], ident[0:64, 0:64]).then_inc(setup_pe, 1)
            for c in range(NC):
                if c % 2 == 0:
                    pe.wait_ge(x_loaded[c // 2], 16)
                if c >= 2:
                    pe.wait_ge(x_ready, c - 1)
                for b in range(NQ):
                    tr = nc.tensor.transpose(ps[c % 2][:, b * P:(b + 1) * P], rows[:, b, c * P:(c + 1) * P], ident[:])
                tr.then_inc(x_turned, 1)
            pe.wait_ge(x_ready, NC)

            with pe.Fori(0, DEPTH) as l:
                h_count = 2 * NC * l + NC

                def project(m, j):
                    products(0, m, j, l, h_hi, h_lo, h_split, h_count)

                project(0, 0)
                pe.wait_ge(sq_added, 2 * NC * l + (NC + CREDIT))
                for t in range(S // BANK):
                    mm = nc.tensor.matmul(ps[2][:, bass.ts(t, BANK)], ones[:], sq_sum[:, bass.ts(t, BANK)],
                                          start=True, stop=True)
                mm.then_inc(ss_done, 1)
                project(0, 1)
                with pe.Fori(1, NPROJ // 2) as m:
                    for j in range(2):
                        project(m, j)

                def turn_v(v):
                    pe.wait_ge(evacuated, NSLAB * l + NPROJ + (v + 1 + CREDIT))
                    if v >= 2:
                        pe.wait_ge(v_stored, NV * l + v - 1)
                    turn(ring[v % 2], ps[2 + v % 2], NQ, vt_turned)

                for v in range(NV):
                    project((NPROJ + v) // 2, v % 2)
                    if v:
                        turn_v(v - 1)
                turn_v(NV - 1)
                def scores(m0, n, pp, i, j, k0, width, pair):
                    pe.wait_ge(staged, 24 * l + 3 * pair + 3)
                    pe.wait_ge(scores_read, m0 + (n - 1 + CREDIT))
                    half = slice(j * HD, (j + 1) * HD)
                    for at in range(0, width, BANK):
                        w = min(BANK, width - at)
                        for p, (q, k) in enumerate(((q_hi, k_hi), (q_hi, k_lo), (q_lo, k_hi))):
                            mm = nc.tensor.matmul(ps[n % 2][:, at:at + w], q[half, pp, i * P:(i + 1) * P],
                                                  k[half, pp, k0 * P + at:k0 * P + at + w],
                                                  start=(p == 0), stop=(p == 2))
                    mm.then_inc(scored, 1)

                def turn_probs(s0, t, slot, blocks, ready, count):
                    pe.wait_ge(ready, count)
                    pe.wait_ge(pt_split, s0 + (t + 1))
                    turn(probs[:, slot], ps[2], blocks, turned)

                def values(s0, t, pp, k0, blocks, e0, e1):
                    pe.wait_ge(pt_split, s0 + (t + 2))
                    pe.wait_ge(o_stored, s0 + (t - 1 + CREDIT))
                    o = ps[3][:, BANK * (t % 2):BANK * (t % 2) + e1 - e0]
                    for b in range(blocks):
                        for p, (a, v) in enumerate(((pt_hi, v_hi), (pt_hi, v_lo), (pt_lo, v_hi))):
                            mm = nc.tensor.matmul(o, a[:, t % 2, b], v[:, pp, k0 + b, e0:e1],
                                                  start=(b == 0 and p == 0), stop=(b == blocks - 1 and p == 2))
                    mm.then_inc(pv_done, 1)

                with pe.Fori(0, 2) as a:
                    s0, m0 = STEPS * l + 16 * a, MAPS * l + 32 * a
                    for t in range(16 + 2):
                        if t == 0:
                            pe.wait_ge(evacuated, NSLAB * l + SPLIT + CREDIT)
                        if t == 1:
                            pe.wait_ge(v_stored, NV * l + NV)
                        if t < 16:
                            for j in range(2):
                                scores(m0, 2 * t + j, t // NQ, t % NQ, j, 0, (t % NQ + 1) * P, 2 * a + t // NQ)
                        if t >= 2:
                            u = t - 2
                            values(s0, u, u // NQ, 0, u % NQ + 1, 0, P)
                        if 1 <= t < 17:
                            u = t - 1
                            turn_probs(s0, u, (2 * u) % 4, u % NQ + 1, combined, s0 + (u + 1))

                pe.wait_ge(cum_ready, l + 1)
                pe.wait_ge(scores_read, MAPS * l + (64 + CREDIT))
                for h in range(CH):
                    if h >= 2:
                        pe.wait_ge(cum_out, 5 * l + h - 1)
                    pick = ident[96:P, F_ROW + h:F_ROW + h + 1].to_broadcast([32, P])
                    for t in range(S // BANK):
                        mm = nc.tensor.matmul(ps[h % 2][:, bass.ts(t, BANK)], pick, raw[96:P, 15, bass.ts(t, BANK)],
                                              start=True, stop=True)
                    mm.then_inc(cum_ps, 1)
                for b in range(NQ):
                    tr = nc.tensor.transpose(ps[2][:, b * 32:(b + 1) * 32], raw[96:P, 15, b * P:(b + 1) * P],
                                             ident[96:P, 96:P])
                tr.then_inc(cum_ps, 1)
                pe.wait_ge(cum_out, 5 * l + 5)

                for grp in "BC":
                    s0, m0 = STEPS * l + STEP0[grp], MAPS * l + MAP0[grp]
                    q0 = 4 if grp == "B" else 6

                    def window(t):
                        i = (t // 2) % NQ
                        blocks = i + 1 if grp == "C" else min(i + 1, 2)
                        return i, i + 1 - blocks, blocks

                    for t in range(32 + 2):
                        if t < 32:
                            i, k0, blocks = window(t)
                            scores(m0, t, t // 16, i, t % 2, k0, blocks * P, q0 + t // 16)
                        if t >= 2:
                            u = t - 2
                            i, k0, blocks = window(u)
                            values(s0, u, u // 16, k0, blocks, (u % 2) * HD, (u % 2 + 1) * HD)
                        if 1 <= t < 33:
                            u = t - 1
                            i, k0, blocks = window(u)
                            turn_probs(s0, u, u % 4, blocks, exp_done, m0 + (u + 1))

                with pe.Fori(0, NC // 2) as m:
                    for j in range(2):
                        pe.wait_ge(y_ready, NC * l + 2 * m + (j + 1))
                        pe.wait_ge(mix_split, NC * l + 2 * m + (j - 1 + CREDIT))
                        turn(turn_in[j], ps[j], NQ, y_turned)
                with pe.Fori(0, NOUT // 2) as m:
                    for j in range(2):
                        products(1, m, j, l, mix_hi, mix_lo, mix_split, NC * l + (NC + CREDIT))

                def up(g, m, j):
                    products(1, NC * g + m + NC // 2, j, l, h_hi, h_lo, h_split, h_count + NC)

                def down(g, m, j):
                    products(1, NC * g + m + NC, j, l, u_hi, u_lo, u_split, 4 * NC * l + NC * g + NC)

                up(0, 0, 0)
                pe.wait_ge(sq_added, 2 * NC * l + (2 * NC + CREDIT))
                for t in range(S // BANK):
                    mm = nc.tensor.matmul(ps[2][:, bass.ts(t, BANK)], ones[:], sq_sum[:, bass.ts(t, BANK)],
                                          start=True, stop=True)
                mm.then_inc(ss_done, 1)
                up(0, 0, 1)
                with pe.Fori(1, NC // 2) as m:
                    for j in range(2):
                        up(0, m, j)
                with pe.Fori(0, NC // 2) as m:
                    for j in range(2):
                        down(0, m, j)
                with pe.Fori(1, GROUPS) as g:
                    with pe.Fori(0, NC // 2) as m:
                        for j in range(2):
                            up(g, m, j)
                    with pe.Fori(0, NC // 2) as m:
                        for j in range(2):
                            down(g, m, j)

            sum_squares(2 * DEPTH + 1)
            for c in range(NC):
                pe.wait_ge(y_ready, NC * DEPTH + c + 1)
                if c >= 2:
                    pe.wait_ge(mix_hi_done, NC * DEPTH + c - 1)
                turn(turn_in[c % 2], ps[c % 2], NQ, y_turned)


_INS = ["x", "w_in", "a_lambda", "a_subln", "b_sinks", "c_fbias", "w_out", "g_mix", "g_mlp", "w_up", "w_down", "g_final"]


def kernel(**inputs):
    import concourse.bacc as _bacc
    from concourse.bass_utils import run_bass_kernel_spmd as _run

    nc = _bacc.Bacc("TRN2", target_bir_lowering=False, num_devices=1)
    arrays, args = {}, []
    for name in _INS:
        a = np.ascontiguousarray(inputs[name])
        arrays[f"in_{name}_dram"] = a
        args.append(nc.dram_tensor(f"in_{name}_dram", a.shape, mybir.dt.from_np(a.dtype), kind="ExternalInput").ap())
    shape = inputs["x"].shape
    args.append(nc.dram_tensor("out_0_dram", shape, F32, kind="ExternalOutput").ap())
    hybrid_encoder(nc, *args)
    r = _run(nc, [arrays], core_ids=[0])
    return r.results[0]["out_0_dram"]
```

```python
import math
from contextlib import ExitStack

import numpy as np

import concourse.bass as bass
from concourse import mybir

F32 = mybir.dt.float32
F32R = mybir.dt.float32r
ALU = mybir.AluOpType
ACT = mybir.ActivationFunctionType
AX = mybir.AxisListType

P = 128
BANK = 512
KB = 1024


def hybrid_encoder(nc, x, w_in, a_lambda, a_subln, b_sinks, c_fbias, w_out, g_mix, g_mlp,
                   w_up, w_down, g_final, out):
    _, S, D = x.shape
    DEPTH = w_in.shape[0]
    HD = a_lambda.shape[2]
    AH, BH, CH = 4, b_sinks.shape[1], c_fbias.shape[1]
    F = w_up.shape[2]
    CHUNK = 64
    EPS = 1e-5
    NEG = -1e30
    NC = D // P
    NQ = S // P
    GROUPS = F // D
    assert (S, D, HD, F) == (1024, 1024, 64, 4096) and NC == 8 and NQ == 8

    PAIRS = 8
    SPLIT = 1 + 3 * (PAIRS - 1) + 1
    NPART = SPLIT - 1
    NOUT = NC
    NSLAB = SPLIT + NOUT + GROUPS * 2 * NC
    OFF_AK = AH * 2 * HD
    OFF_AV = 2 * OFF_AK
    OFF_BQ = OFF_AV + AH * 2 * HD
    OFF_BK = OFF_BQ + BH * HD
    OFF_BV = OFF_BK + BH * HD // 2
    OFF_CQ = OFF_BV + BH * HD // 2
    OFF_CK = OFF_CQ + CH * HD
    OFF_CV = OFF_CK + CH * HD
    OFF_CF = OFF_CV + CH * HD
    D_IN = OFF_CF + CH
    assert D_IN == w_in.shape[2]
    F_ROW = P - CH
    C0, B0 = AH, AH + 2
    PROJ_COLS = [D_IN - P]
    for n in range(AH):
        PROJ_COLS += [P * n, OFF_AK + P * n, OFF_AV + P * n]
    for n in range(2):
        PROJ_COLS += [OFF_CQ + P * n, OFF_CK + P * n, OFF_CV + P * n]
    PROJ_COLS += [None, OFF_BK, OFF_BV, None]
    assert len(PROJ_COLS) == SPLIT
    CREDIT = 2

    SLOPE_A = [2.0 ** (-8.0 * (2 * h + 1) / (AH + BH)) for h in range(AH)]
    SLOPE_B = [2.0 ** (-8.0 * (2 * h + 2) / (AH + BH)) for h in range(BH)]
    SLOPES = [(s, s) for s in SLOPE_A] + [(1.0, 1.0)] * 2 + [(SLOPE_B[p], SLOPE_B[2 + p]) for p in range(2)]
    STEPS = 96
    MAPS = 128

    PIECES = {"A": [4, 4, 3, 3, 2, 3, 3, 2], "C": [2] * 8 + [1] * 8, "B": [1] * 8 + [0] * 8}

    class Run:
        def __init__(self, groups, parity):
            self.parity = parity
            self.steps, self.pieces, self.ended = [], [], []
            self.pair_start = []
            at = 0
            for pp, grp in enumerate(groups):
                last = grp == "B" and pp == len(groups) - 1
                for u in range(NQ if grp == "A" else 2 * NQ):
                    self.steps.append((grp, pp, u, None) if grp == "A" else (grp, pp, u // 2, u % 2))
                    self.pair_start.append(u == 0)
                    count = 0 if last else PIECES[grp][u]
                    self.pieces.append([(k // NC, k % NC) for k in range(at, at + count)])
                    at += count
                    self.ended.append(at // NC - 1 if count and at // NC > (at - count) // NC else None)
            self.n = len(self.steps)

        def ends(self, t):
            return self.ended[t] if 0 <= t < self.n else None

    RUN_A, RUN_C, RUN_CB = Run("AA", 0), Run("C", 0), Run("CBB", 1)

    MIX_CHUNK = [0, 1, 2, 3, 6, 7, 4, 5]

    def window(grp, i):
        blocks = min(i + 1, 2) if grp == "B" else i + 1
        return i + 1 - blocks, blocks

    x_rows = x[0].rearrange("(b p) d -> p b d", p=P)
    out_rows = out[0].rearrange("(b p) d -> p b d", p=P)
    x_saved = nc.dram_tensor("x_saved", (P, NC * S), F32, kind="Internal").ap()

    with ExitStack() as ctx:
        def sem(name):
            return ctx.enter_context(nc.semaphore(name))

        base = (nc.sbuf_base + 31) // 32 * 32

        def place(name, shape, offset, dtype=F32):
            return nc.alloc_sbuf_tensor_at(name, shape, dtype, offset=base + offset)

        W_AT, H_AT, PART_AT, PROBS_AT, PT_AT = 0, 20 * KB, 84 * KB, 132 * KB, 148 * KB
        TMP_AT, RMS_AT, GATE_AT, X_AT, T_AT = 156 * KB, 160 * KB, 164 * KB, 168 * KB, 200 * KB
        w_raw = place("w_raw", [P, NC, P], W_AT)
        w_hi = place("w_hi", [P, 2, NC, P], W_AT + 4 * KB, F32R)
        w_lo = place("w_lo", [P, 2, NC, P], W_AT + 12 * KB, F32R)
        h_hi = place("h_hi", [P, NC, S], H_AT, F32R)
        h_lo = place("h_lo", [P, NC, S], H_AT + 32 * KB, F32R)
        q_hi = place("q_hi", [P, 2, S], PART_AT, F32R)
        q_lo = place("q_lo", [P, 2, S], PART_AT + 8 * KB, F32R)
        k_hi = place("k_hi", [P, 2, S], PART_AT + 16 * KB, F32R)
        k_lo = place("k_lo", [P, 2, S], PART_AT + 24 * KB, F32R)
        v_hi = place("v_hi", [P, 2, NQ, P], PART_AT + 32 * KB, F32R)
        v_lo = place("v_lo", [P, 2, NQ, P], PART_AT + 40 * KB, F32R)
        probs = place("probs", [P, 4, S], PROBS_AT)
        pt_hi = place("pt_hi", [P, NQ, P], PT_AT, F32R)
        pt_lo = place("pt_lo", [P, NQ, P], PT_AT + 4 * KB, F32R)
        mix_hi = place("mix_hi", [P, NC, S], PART_AT, F32R)
        mix_lo = place("mix_lo", [P, NC, S], PART_AT + 32 * KB, F32R)
        u_hi = place("u_hi", [P, NC, S], PART_AT, F32R)
        u_lo = place("u_lo", [P, NC, S], PART_AT + 32 * KB, F32R)
        rows = place("rows", [P, NQ, D], PART_AT)
        ring = [place("ring0", [P, S], PT_AT), place("ring1", [P, S], PT_AT + 4 * KB)]
        turn_in = [ring[0][:], ring[1][:]]
        gate_tmp = place("gate_tmp", [P, S], PT_AT)
        sq_sum = place("sq_sum", [P, S], TMP_AT)
        part = place("part", [P, S], TMP_AT)
        inv_rms = place("inv_rms", [P, S], RMS_AT)
        cum = place("cum", [P, S], GATE_AT)
        lam_raw = place("lam_raw", [P, DEPTH * 4 * HD], GATE_AT)
        lam_prod_at = place("lam_prod", [P, DEPTH * 2 * HD], RMS_AT)
        o_out = place("o_out", [P, PAIRS, S], X_AT)
        xt = place("xt", [P, NC, S], X_AT)
        cursor = [T_AT]

        def small(name, shape, dtype=F32):
            t = place(name, shape, cursor[0], dtype)
            cursor[0] += (4 * int(np.prod(shape[1:])) + 31) // 32 * 32
            assert base + cursor[0] <= nc.sbuf_usable_end
            return t

        ident = small("ident", [P, P])
        ones = small("ones", [P, P])
        far = small("far", [P, S])
        near = small("near", [P, 2 * P])
        causal = small("causal", [P, P])
        NPAR = (2 * DEPTH + 1) * NC
        param = small("param", [P, 64])
        mix_gain = small("mix_gain", [P, DEPTH * NC])
        q_scale = small("q_scale", [P, PAIRS])
        slope = small("slope", [P, 16])
        neg_slope = small("neg_slope", [P, 16])
        sink_raw = small("sink_raw", [P, DEPTH * BH])
        sink = small("sink", [P, DEPTH * 4])
        neg_lam = small("neg_lam", [P, DEPTH])
        lam_dot = small("lam_dot", [P, DEPTH * 2])
        eps = small("eps", [P, 1])
        row_max = small("row_max", [P, 8])
        neg_max = small("neg_max", [P, 8])
        row_sum = small("row_sum", [P, 8])
        sink_exp = small("sink_exp", [P, 8])
        inv_sum = small("inv_sum", [P, 8])
        lam_ratio = small("lam_ratio", [P, 8])
        o_sq = small("o_sq", [P, AH * NQ])
        o_inv = small("o_inv", [P, AH * NQ])
        o_sq_now = small("o_sq_now", [P, 2 * NQ])
        slope_now = small("slope_now", [P, 4])
        wait_slot = small("wait_slot", [P, 1])
        cum_q = small("cum_q", [P, NQ * CH])
        par_raw = place("par_raw", [64, P], TMP_AT)

        ps = [ctx.enter_context(nc.psum_tensor(f"ps{i}", [P, 2 * BANK], F32)) for i in range(4)]

        w_loaded = sem("w_loaded")
        w_hi_done = sem("w_hi_done")
        w_split = sem("w_split")
        slab_done = sem("slab_done")
        evacuated = sem("evacuated")
        x_loaded = [sem(f"x_loaded{i}") for i in range(4)]
        x_turned = sem("x_turned")
        x_ready = sem("x_ready")
        squared = sem("squared")
        sq_added = sem("sq_added")
        h_hi_done = sem("h_hi_done")
        h_split = sem("h_split")
        ss_done = sem("ss_done")
        rms_done = sem("rms_done")
        relu_sq = sem("relu_sq")
        u_split = sem("u_split")
        part_hi = sem("part_hi")
        split_done = sem("split_done")
        v_turned = sem("v_turned")
        x_spilled = sem("x_spilled")
        x_back = [sem("x_back0"), sem("x_back1")]
        gate_log = sem("gate_log")
        cum_ready = sem("cum_ready")
        cum_ps = sem("cum_ps")
        cum_out = sem("cum_out")
        scored = sem("scored")
        scores_read = sem("scores_read")
        max_done = sem("max_done")
        bias_done = sem("bias_done")
        exp_done = sem("exp_done")
        combined = sem("combined")
        turned = sem("turned")
        pt_hi_done = sem("pt_hi_done")
        pt_split = sem("pt_split")
        pv_done = sem("pv_done")
        o_stored = sem("o_stored")
        o_rms = sem("o_rms")
        y_ready = sem("y_ready")
        y_turned = sem("y_turned")
        mix_hi_done = sem("mix_hi_done")
        mix_split = sem("mix_split")
        setup_pool = sem("setup_pool")
        setup_dve = sem("setup_dve")
        setup_act = sem("setup_act")
        setup_pe = sem("setup_pe")
        par_loaded = sem("par_loaded")
        bc_loaded = sem("bc_loaded")
        out_done = sem("out_done")

        block = ctx.enter_context(nc.Block())

        def w_dram(matrix, l):
            return matrix[l].rearrange("(c p) n -> p c n", p=P)

        def slab_no(region, m, j):
            return 2 * m + j + (SPLIT if region else 0)

        def ring_free(region, m, j):
            if region and isinstance(m, int) and m == 0:
                return SPLIT + CREDIT
            return slab_no(region, m, j) - 1 + CREDIT

        @block.sync
        def _(sp):
            for i in range(4):
                w = D // 4
                sp.dma_start(rows[:, :, i * w:(i + 1) * w], x_rows[:, :, i * w:(i + 1) * w]).then_inc(x_loaded[i], 16)
            sp.wait_ge(setup_pool, 1)
            r = 0
            for l in range(DEPTH):
                for g in (g_mix, g_mlp):
                    sp.dma_start(par_raw[r:r + NC, :], g[l].rearrange("(c p) -> c p", p=P)).then_inc(par_loaded, 16)
                    r += NC
            sp.dma_start(par_raw[r:r + NC, :], g_final.rearrange("(c p) -> c p", p=P)).then_inc(par_loaded, 16)
            sp.dma_start(par_raw[NPAR:NPAR + DEPTH, :], a_subln).then_inc(par_loaded, 16)
            sp.dma_start(par_raw[NPAR + DEPTH:NPAR + 2 * DEPTH, F_ROW:P], c_fbias).then_inc(par_loaded, 16)
            sp.dma_start(lam_raw[:], a_lambda.rearrange("(o l) k d -> o (l k d)", o=1).to_broadcast([P, DEPTH * 4 * HD])).then_inc(bc_loaded, 16)
            sp.dma_start(sink_raw[:], b_sinks.rearrange("(o l) h -> o (l h)", o=1).to_broadcast([P, DEPTH * BH])).then_inc(bc_loaded, 16)

            def load(l, s, parts):
                sp.wait_ge(w_split, NSLAB * l + s + CREDIT)
                for dst, src in parts:
                    sp.dma_start(dst, src).then_inc(w_loaded, 16)

            def halves(src):
                h = NC // 2
                return [(w_raw[:, h:NC], src[:, h:NC]), (w_raw[:, 0:h], src[:, 0:h])]

            with sp.Fori(0, DEPTH) as l:
                win = w_dram(w_in, l)

                def load_proj(s):
                    c0 = PROJ_COLS[s]
                    if c0 is None:
                        at = OFF_BQ + (HD if s == SPLIT - 1 else 0)
                        parts = [(w_raw[:, :, g * HD:(g + 1) * HD],
                                  win[:, :, at + 2 * HD * g:at + 2 * HD * g + HD]) for g in range(2)]
                    else:
                        parts = halves(win[:, :, c0:c0 + P])
                    load(l, s, parts)

                for s in range(2):
                    load_proj(s)
                sp.wait_ge(h_split, 2 * NC * l + NC)
                sp.dma_start(x_saved, xt[:].rearrange("p c s -> p (c s)")).then_inc(x_spilled, 16)
                for s in range(2, SPLIT):
                    load_proj(s)
                wo = w_dram(w_out, l).rearrange("p c (m j n) -> m j p c n", j=2, n=P)
                for j in range(2):
                    load(l, SPLIT + j, halves(wo[0, j]))
                half = NC // 2
                for i in range(2):
                    sp.wait_ge(y_ready, NC * l + half * (i + 1))
                    sp.dma_start(xt[:, half * i:half * (i + 1)].rearrange("p c s -> p (c s)"),
                                 x_saved[:, half * S * i:half * S * (i + 1)]).then_inc(x_back[i], 16)
                with sp.Fori(1, NOUT // 2) as m:
                    for j in range(2):
                        load(l, slab_no(1, m, j), halves(wo[m, j]))
                up = w_dram(w_up, l).rearrange("p c (g m j n) -> g m j p c n", g=GROUPS, j=2, n=P)
                down = w_down[l].rearrange("(g c p) (m j n) -> g m j p c n", p=P, c=NC, j=2, n=P)
                with sp.Fori(0, GROUPS) as g:
                    with sp.Fori(0, NC // 2) as m:
                        for j in range(2):
                            load(l, slab_no(1, NC * g + (m + NC // 2), j), halves(up[g, m, j]))
                    with sp.Fori(0, NC // 2) as m:
                        for j in range(2):
                            load(l, slab_no(1, NC * g + (m + NC), j), halves(down[g, m, j]))
            for i in range(4):
                w = D // 4
                sp.wait_ge(mix_hi_done, NC * DEPTH + 2 * (i + 1))
                sp.dma_start(out_rows[:, :, i * w:(i + 1) * w], rows[:, :, i * w:(i + 1) * w]).then_inc(out_done, 16)
            sp.wait_ge(out_done, 4 * 16)

        @block.gpsimd
        def _(pool):
            pool.memset(par_raw[:], 0.0).then_inc(setup_pool, 1)
            pool.memset(ident[:], 0.0).then_inc(setup_pool, 1)
            pool.memset(causal[:], 0.0).then_inc(setup_pool, 1)
            pool.iota(far[:], [[-1, S]], base=S - P, channel_multiplier=1,
                      allow_small_or_imprecise_dtypes=True).then_inc(setup_pool, 1)
            pool.iota(near[:], [[-1, 2 * P]], base=P, channel_multiplier=1,
                      allow_small_or_imprecise_dtypes=True).then_inc(setup_pool, 1)
            pool.wait_ge(setup_pool, 5)
            pool.affine_select(out=ident[:], in_=ident[:], compare_op=ALU.not_equal, fill=1.0, base=0,
                               pattern=[[-1, P]], channel_multiplier=1).then_inc(setup_pool, 1)
            pool.affine_select(out=causal[:], in_=causal[:], compare_op=ALU.is_ge, fill=NEG, base=0,
                               pattern=[[-1, P]], channel_multiplier=1).then_inc(setup_pool, 1)
            def add_squares(n0, c, slot):
                pool.wait_ge(squared, n0 + (c + 1))
                if isinstance(c, int) and c == 0:
                    nc.gpsimd.tensor_tensor(sq_sum[:], ring[slot][:], ones[:, 0:1].to_broadcast([P, S]),
                                            ALU.mult).then_inc(sq_added, 1)
                else:
                    pool.wait_ge(sq_added, n0 + (c + CREDIT))
                    nc.gpsimd.tensor_tensor(sq_sum[:], sq_sum[:], ring[slot][:], ALU.add).then_inc(sq_added, 1)

            def norm_squares(n0):
                for c in range(NC):
                    add_squares(n0, c, c % 2)

            pool.sem_inc(sq_added, CREDIT)
            norm_squares(0)
            with pool.Fori(0, DEPTH) as l:
                norm_squares(2 * NC * l + NC)
                norm_squares(2 * NC * l + 2 * NC)

        @block.scalar
        def _(act):
            def split_w(l, region, m, j):
                act.wait_ge(w_loaded, 32 * NSLAB * l + 32 * slab_no(region, m, j) + 32)
                act.wait_ge(slab_done, NSLAB * l + ring_free(region, m, j))
                nc.scalar.activation(w_hi[:, j], w_raw[:], ACT.Copy).then_inc(w_hi_done, 1)

            def prepare(n0, gain, c, slot):
                act.wait_ge(sq_added, n0 + c + 1)
                nc.scalar.activation(ring[slot][:], xt[:, c], ACT.Square).then_inc(squared, 1)
                nc.scalar.activation(h_hi[:, c], xt[:, c], ACT.Copy,
                                     scale=param[:, bass.ds(gain, 1)]).then_inc(h_hi_done, 1)

            def root_mean_square(n):
                act.wait_ge(ss_done, n)
                nc.scalar.activation(inv_rms[:], ps[2][:], ACT.Sqrt, bias=eps[:, 0:1], scale=1.0 / D).then_inc(rms_done, 1)

            act.sem_inc(o_stored, CREDIT)
            act.wait_ge(setup_dve, 1)
            nc.scalar.activation(lam_dot[:], lam_dot[:], ACT.Exp).then_inc(setup_act, 1)
            for c in range(NC):
                act.wait_ge(x_ready, c + 1)
                prepare(0, c, c, c % 2)

            with act.Fori(0, DEPTH) as l:
                def split_proj(s, j):
                    act.wait_ge(w_loaded, 32 * NSLAB * l + 32 * s + 32)
                    act.wait_ge(slab_done, NSLAB * l + s - 1 + CREDIT)
                    nc.scalar.activation(w_hi[:, j], w_raw[:], ACT.Copy).then_inc(w_hi_done, 1)

                def part_high(s, dst):
                    act.wait_ge(evacuated, NSLAB * l + s + (1 + CREDIT))
                    nc.scalar.activation(dst, part[:], ACT.Copy).then_inc(part_hi, 1)

                split_proj(0, 0)
                split_proj(1, 1)
                root_mean_square(2 * l + 1)
                split_proj(2, 0)
                act.wait_ge(evacuated, NSLAB * l + (1 + CREDIT))
                g_in, g_tmp = cum[96:P], gate_tmp[96:P]
                bias = param[96:P, bass.ds(l + (NPAR + DEPTH), 1)]
                nc.scalar.activation(g_tmp, g_in, ACT.Abs, bias=bias)
                act.drain()
                nc.scalar.activation(g_tmp, g_tmp, ACT.Exp, scale=-1.0)
                act.drain()
                nc.scalar.activation(g_tmp, g_tmp, ACT.Ln, bias=1.0).then_inc(gate_log, 1)
                split_proj(3, 1)
                part_high(1, q_hi[:, 0])
                split_proj(4, 0)
                part_high(2, k_hi[:, 0])

                def spread_out(head, n, p):
                    act.wait_ge(cum_ps, 5 * l + n)
                    nc.scalar.activation(o_out[:, B0 + head % 2], ps[p][:], ACT.Copy, scale=-1.0).then_inc(cum_out, 1)

                act.wait_ge(x_spilled, 16 * l + 16)
                spread_out(0, 1, 3)
                act.wait_ge(cum_ps, 5 * l + 2)
                nc.scalar.activation(cum_q[:].rearrange("p (b h) -> p b h", h=CH),
                                     ps[2][:, 0:NQ * 32].rearrange("p (b h) -> p b h", h=32)[:, :, 32 - CH:32],
                                     ACT.Copy).then_inc(cum_out, 1)
                split_proj(5, 1)
                spread_out(1, 3, 2)

                def forget_bias(t, run, s0):
                    grp, pp, i, j = run.steps[t]
                    if grp != "C" or i == 0:
                        return
                    if t >= 4:
                        act.wait_ge(turned, s0 + (t - 3 + CREDIT))
                    h = 2 * run.parity + j
                    nc.scalar.activation(probs[:, t % 4, 0:i * P], o_out[:, B0 + j, 0:i * P], ACT.Identity,
                                         bias=cum_q[:, i * CH + h:i * CH + h + 1]).then_inc(bias_done, 1)

                def probs_hi(s0, t, blocks):
                    act.wait_ge(turned, s0 + (t + 1 + CREDIT))
                    nc.scalar.activation(pt_hi[:, 0:blocks], ps[2][:, 0:blocks * P].rearrange("p (b q) -> p b q", q=P),
                                         ACT.Copy).then_inc(pt_hi_done, 1)

                def store_o(s0, t, pair, i, j, n):
                    act.wait_ge(pv_done, s0 + (t + 1))
                    act.wait_ge(combined, s0 + (t + 1))
                    w = P if j is None else HD
                    at = i * P + (0 if j is None else HD * j)
                    o = ps[3][:, BANK * (t % 2):BANK * (t % 2) + w]
                    inv = inv_sum[:, n % 8:n % 8 + 1]
                    if j is None:
                        nc.scalar.activation(ps[3][:, BANK * (t % 2) + P:BANK * (t % 2) + 2 * P], o, ACT.Square, scale=inv,
                                             accum_out=o_sq_now[:, t:t + 1])
                    nc.scalar.activation(o_out[:, pair, at:at + w], o, ACT.Copy, scale=inv).then_inc(o_stored, 1)

                def exponentials(m0, n, width, sl, sink_at=None):
                    act.wait_ge(max_done, m0 + (n + 1))
                    e = nc.scalar.activation(probs[:, n % 4, 0:width], probs[:, n % 4, 0:width], ACT.Exp,
                                             bias=neg_max[:, n % 8:n % 8 + 1], scale=sl,
                                             accum_out=row_sum[:, n % 8:n % 8 + 1])
                    if sink_at is not None:
                        e = nc.scalar.activation(sink_exp[:, n % 8:n % 8 + 1], sink[:, bass.ds(sink_at, 1)], ACT.Exp,
                                                 bias=neg_max[:, n % 8:n % 8 + 1], scale=sl)
                    e.then_inc(exp_done, 1)

                def attend(run, s0, m0, pair0, slab0, n_turned):
                    if run is RUN_C or run is RUN_CB:
                        forget_bias(0, run, s0)
                    for t in range(run.n + 2):
                        now = run.steps[t] if t < run.n else None
                        if t >= 2:
                            probs_hi(s0, t - 2, window(run.steps[t - 2][0], run.steps[t - 2][2])[1])
                        if t + 1 < run.n:
                            forget_bias(t + 1, run, s0)

                        def exp_of(k):
                            grp, pp, i, j = now
                            width = window(grp, i)[1] * P
                            if grp == "A":
                                exponentials(m0, 2 * t + k, width, slope_now[:, 2 * pp + k:2 * pp + k + 1])
                            else:
                                at = 2 * (pair0 + pp) + j
                                exponentials(m0, t, width, slope[:, at:at + 1],
                                             4 * l + (2 * (pair0 + pp - B0) + j) if grp == "B" else None)

                        if now:
                            exp_of(0)
                            if run.pair_start[t] and not (now[0] == "B" and now[1] == 2):
                                slot = (run.parity + now[1]) % 2
                                act.wait_ge(v_turned, (PAIRS - 1) * l + n_turned + (now[1] + 1))
                                nc.scalar.activation(v_hi[:, slot], ps[1][:].rearrange("p (b d) -> p b d", d=P),
                                                     ACT.Copy).then_inc(part_hi, 1)
                        k = run.ends(t - 1)
                        if k is not None and k % 3 < 2:
                            slot = (run.parity + 1 + k // 3) % 2
                            part_high(slab0 + k, (q_hi, k_hi)[k % 3][:, slot])
                        if t >= 2:
                            grp, pp, i, j = run.steps[t - 2]
                            store_o(s0, t - 2, pair0 + pp, i, j, 2 * (t - 2) if grp == "A" else t - 2)
                        if now and now[0] == "A":
                            exp_of(1)
                        if k is not None:
                            if not (run is RUN_CB and k >= 2):
                                split_proj(slab0 + (k + 2), (run.parity + k) % 2)
                            elif k == 3:
                                split_w(l, 1, 0, 0)

                with act.Fori(0, 2) as a:
                    nc.scalar.activation(slope_now[:], slope[:, bass.ds(4 * a, 4)], ACT.Copy)
                    act.drain()
                    attend(RUN_A, STEPS * l + 16 * a, MAPS * l + 32 * a, 2 * a, 6 * a + 4, 2 * a)
                    act.drain()
                    nc.scalar.activation(o_sq[:, bass.ts(a, 2 * NQ)], o_sq_now[:], ACT.Copy)
                attend(RUN_C, STEPS * l + 32, MAPS * l + 64, C0, 16, 4)
                act.drain()
                spread_out(2, 4, 0)
                spread_out(3, 5, 2)
                act.drain()
                attend(RUN_CB, STEPS * l + 48, MAPS * l + 80, C0 + 1, 19, 5)

                act.drain()
                nc.scalar.activation(o_inv[:], o_sq[:], ACT.Sqrt, bias=eps[:, 0:1], scale=1.0 / P).then_inc(o_rms, 1)
                for n, c in enumerate(MIX_CHUNK):
                    act.wait_ge(y_turned, NC * l + n + 1)
                    nc.scalar.activation(mix_hi[:, c], ps[n % 2][:], ACT.Copy,
                                         scale=mix_gain[:, bass.ds(NC * l + c, 1)]).then_inc(mix_hi_done, 1)

                def prepared(n0, gain, m_slab, m, j, n_slab):
                    act.wait_ge(evacuated, NSLAB * l + n_slab + (1 + CREDIT))
                    prepare(n0, gain, 2 * m + j, j)

                with act.Fori(0, NOUT // 2) as m:
                    for j in range(2):
                        split_w(l, 1, m + j, 1 - j)
                        prepared(2 * NC * l + NC, 2 * NC * l + NC + 2 * m + j, m, m, j, slab_no(1, m, j))

                def hidden(g, m, j):
                    act.wait_ge(evacuated, NSLAB * l + slab_no(1, NC * g + m + NC // 2, j) + (1 + CREDIT))
                    nc.scalar.activation(ring[j][:], ring[j][:], ACT.Square)
                    act.drain()
                    nc.scalar.activation(u_hi[:, 2 * m + j], ring[j][:], ACT.Copy).then_inc(relu_sq, 1)

                split_w(l, 1, NC // 2, 1)
                root_mean_square(2 * l + 2)
                hidden(0, 0, 0)
                split_w(l, 1, NC // 2 + 1, 0)
                hidden(0, 0, 1)

                def up(g, m):
                    for j in range(2):
                        split_w(l, 1, NC * g + m + (NC // 2 + j), 1 - j)
                        hidden(g, m, j)

                def down(g, m, last):
                    for j in range(2):
                        if not (last and isinstance(m, int) and j == 1):
                            split_w(l, 1, NC * g + m + (NC + j), 1 - j)
                        if last:
                            prepared(2 * NC * l + 2 * NC, 2 * NC * l + 2 * NC + 2 * m + j, m, m, j,
                                     slab_no(1, NC * g + m + NC, j))

                with act.Fori(1, NC // 2) as m:
                    up(0, m)
                with act.Fori(0, NC // 2) as m:
                    down(0, m, False)
                with act.Fori(1, GROUPS - 1) as g:
                    with act.Fori(0, NC // 2) as m:
                        up(g, m)
                    with act.Fori(0, NC // 2) as m:
                        down(g, m, False)
                with act.Fori(0, NC // 2) as m:
                    up(GROUPS - 1, m)
                with act.Fori(0, NC // 2 - 1) as m:
                    down(GROUPS - 1, m, True)
                down(GROUPS - 1, NC // 2 - 1, True)

            root_mean_square(2 * DEPTH + 1)
            for c in range(NC):
                act.wait_ge(y_turned, NC * DEPTH + c + 1)
                nc.scalar.activation(rows[:, :, c * P:(c + 1) * P], ps[c % 2][:].rearrange("p (b d) -> p b d", d=P),
                                     ACT.Copy).then_inc(mix_hi_done, 1)

        @block.vector
        def _(dve):
            V = nc.vector

            V.memset(ones[:], 1.0)
            V.memset(eps[:], EPS)
            for q, (s_lo, s_hi) in enumerate(SLOPES):
                for j, s in enumerate((s_lo, s_hi)):
                    V.memset(slope[:, 2 * q + j:2 * q + j + 1], s)
                    V.memset(neg_slope[:, 2 * q + j:2 * q + j + 1], -s)
                    V.memset(q_scale[j * HD:(j + 1) * HD, q:q + 1], HD ** -0.5 / s)
            V.memset(mix_gain[:], 1.0)
            dve.wait_ge(setup_pool, 5)
            for t in (far, near):
                V.scalar_tensor_tensor(out=t[:], in0=t[:], scalar=-1.0, in1=t[:], op0=ALU.mult, op1=ALU.min)
            V.drain()
            for t, w in ((far, S), (near, 2 * P)):
                V.memset(t[0:CHUNK, w - CHUNK:w], NEG)
            V.memset(near[:, 0:CHUNK], NEG)
            V.memset(near[CHUNK:P, CHUNK:P], NEG)
            dve.wait_ge(bc_loaded, 32)
            lam4 = lam_raw[:].rearrange("p (a k d) -> p a k d", k=2, d=HD)
            lam_prod = lam_prod_at[:].rearrange("p (a d) -> p a d", d=HD)
            V.tensor_tensor(lam_prod, lam4[:, :, 0], lam4[:, :, 1], ALU.mult)
            V.drain()
            V.tensor_reduce(lam_dot[:], lam_prod, AX.X, ALU.add).then_inc(setup_dve, 1)
            for l in range(DEPTH):
                for p in range(2):
                    for j in range(2):
                        at = 4 * l + 2 * p + j
                        h = 2 * j + p
                        V.tensor_scalar(sink[:, at:at + 1], sink_raw[:, l * BH + h:l * BH + h + 1], 1.0 / SLOPE_B[h],
                                        None, ALU.mult)
            dve.wait_ge(setup_act, 1)
            for l in range(DEPTH):
                lam_init = 0.8 - 0.6 * math.exp(-0.3 * l)
                V.tensor_tensor(neg_lam[:, l:l + 1], lam_dot[:, 2 * l + 1:2 * l + 2], lam_dot[:, 2 * l:2 * l + 1],
                                ALU.subtract)
                V.drain()
                V.tensor_scalar(neg_lam[:, l:l + 1], neg_lam[:, l:l + 1], -lam_init, None, ALU.add)
            dve.wait_ge(setup_pe, 1)
            V.tensor_copy(param[:], ps[3][:, 0:64])
            V.drain()
            for l in range(DEPTH):
                lam_init = 0.8 - 0.6 * math.exp(-0.3 * l)
                for c in range(AH):
                    V.tensor_scalar(mix_gain[:, l * NC + c:l * NC + c + 1], param[:, NPAR + l:NPAR + l + 1],
                                    1.0 - lam_init, None, ALU.mult)
            V.drain()
            dve.sem_inc(w_split, CREDIT)
            dve.sem_inc(evacuated, CREDIT)
            dve.sem_inc(scores_read, CREDIT)
            dve.sem_inc(pt_split, 1)
            dve.sem_inc(mix_split, CREDIT)

            def split_w(l, region, m, j):
                dve.wait_ge(w_hi_done, NSLAB * l + slab_no(region, m, j) + 1)
                V.tensor_tensor(w_lo[:, j], w_raw[:], w_hi[:, j].bitcast(F32), ALU.subtract).then_inc(w_split, 1)

            def result(l, region, m, j):
                dve.wait_ge(slab_done, NSLAB * l + slab_no(region, m, j) + (1 + CREDIT))
                return ps[j][:]

            def h_low(n0, gain, c):
                dve.wait_ge(h_hi_done, n0 + c + 1)
                V.scalar_tensor_tensor(out=h_lo[:, c], in0=xt[:, c], scalar=param[:, bass.ds(gain, 1)],
                                       in1=h_hi[:, c].bitcast(F32), op0=ALU.mult, op1=ALU.subtract).then_inc(h_split, 1)

            def invert_rms(n):
                dve.wait_ge(rms_done, n)
                V.reciprocal(inv_rms[:], inv_rms[:])
                V.drain()

            for c in range(NC):
                dve.wait_ge(x_turned, c + 1)
                V.tensor_copy(xt[:, c], ps[c % 2][:]).then_inc(x_ready, 1)
                if c:
                    h_low(0, c - 1, c - 1)
            h_low(0, NC - 1, NC - 1)

            with dve.Fori(0, DEPTH) as l:
                def split_proj(s, j):
                    dve.wait_ge(w_hi_done, NSLAB * l + s + 1)
                    V.tensor_tensor(w_lo[:, j], w_raw[:], w_hi[:, j].bitcast(F32), ALU.subtract).then_inc(w_split, 1)

                def part_low(s, lo, hi, src):
                    dve.wait_ge(part_hi, NPART * l + s)
                    V.tensor_tensor(lo, src, hi.bitcast(F32), ALU.subtract).then_inc(split_done, 1)

                def evacuate(s, pair, kind, p):
                    dve.wait_ge(slab_done, NSLAB * l + s + (1 + CREDIT))
                    if kind:
                        dve.wait_ge(split_done, NPART * l + (s - 1))
                    if kind == 0:
                        e = V.scalar_tensor_tensor(out=part[:], in0=ps[p][:], scalar=q_scale[:, bass.ds(pair, 1)],
                                                   in1=inv_rms[:], op0=ALU.mult, op1=ALU.mult)
                    else:
                        e = V.tensor_tensor(part[:], ps[p][:], inv_rms[:], ALU.mult)
                    e.then_inc(evacuated, 1)

                split_proj(0, 0)
                split_proj(1, 1)
                invert_rms(2 * l + 1)
                dve.wait_ge(slab_done, NSLAB * l + 1 + CREDIT)
                V.tensor_tensor(cum[96:P], ps[0][96:P], inv_rms[96:P], ALU.mult).then_inc(evacuated, 1)
                split_proj(2, 0)
                dve.wait_ge(gate_log, l + 1)
                g_in, g_tmp = cum[96:P], gate_tmp[96:P]
                V.tensor_scalar(g_in, g_in, param[96:P, bass.ds(l + (NPAR + DEPTH), 1)], 0.0, ALU.add, ALU.min)
                V.drain()
                V.tensor_tensor(g_tmp, g_in, g_tmp, ALU.subtract)
                V.drain()
                V.tensor_tensor_scan(g_in, ones[96:P, 0:1].to_broadcast([32, S]), g_tmp, 0.0, ALU.mult, ALU.add)\
                    .then_inc(cum_ready, 1)
                evacuate(1, 0, 0, 1)
                split_proj(3, 1)
                part_low(1, q_lo[:, 0], q_hi[:, 0], part[:])
                evacuate(2, 0, 1, 0)
                split_proj(4, 0)
                part_low(2, k_lo[:, 0], k_hi[:, 0], part[:])
                evacuate(3, 0, 2, 1)
                split_proj(5, 1)

                def probs_lo(s0, t, blocks):
                    dve.wait_ge(pt_hi_done, s0 + (t + 1))
                    V.tensor_tensor(pt_lo[:, 0:blocks], ps[2][:, 0:blocks * P].rearrange("p (b q) -> p b q", q=P),
                                    pt_hi[:, 0:blocks].bitcast(F32), ALU.subtract).then_inc(pt_split, 1)

                def biased_max(s0, m0, t, back, n, width, bias, sc, sink_at=None):
                    dve.wait_ge(scored, m0 + (n + 1))
                    dve.wait_ge(turned, s0 + (t - back + CREDIT))
                    V.memset(wait_slot[:], 0.0)
                    at = n % 8
                    V.tensor_tensor_reduce(out=probs[:, n % 4, 0:width], in0=ps[0][:, 0:width], in1=bias, scale=1.0,
                                           scalar=-3e38, op0=ALU.add, op1=ALU.max, accum_out=row_max[:, at:at + 1])\
                        .then_inc(scores_read, 1)
                    V.drain()
                    neg = neg_slope[:, bass.ds(sc, 1)]
                    if sink_at is None:
                        e = V.tensor_scalar(neg_max[:, at:at + 1], row_max[:, at:at + 1], neg, None, ALU.mult)
                    else:
                        e = V.tensor_scalar(neg_max[:, at:at + 1], row_max[:, at:at + 1],
                                            sink[:, bass.ds(sink_at, 1)], neg, ALU.max, ALU.mult)
                    e.then_inc(max_done, 1)

                def combine(m0, t, width):
                    dve.wait_ge(exp_done, m0 + (2 * t + 2))
                    c, s = (2 * t) % 8, (2 * t) % 4
                    V.reciprocal(inv_sum[:, c:c + 2], row_sum[:, c:c + 2])
                    V.drain()
                    V.tensor_scalar(lam_ratio[:, c:c + 1], inv_sum[:, c + 1:c + 2], row_sum[:, c:c + 1],
                                    neg_lam[:, bass.ds(l, 1)], ALU.mult, ALU.mult)
                    V.drain()
                    V.scalar_tensor_tensor(out=probs[:, s, 0:width], in0=probs[:, s + 1, 0:width],
                                           scalar=lam_ratio[:, c:c + 1], in1=probs[:, s, 0:width],
                                           op0=ALU.mult, op1=ALU.add).then_inc(combined, 1)

                def invert_sum(m0, t, with_sink):
                    dve.wait_ge(exp_done, m0 + (t + 1))
                    c = t % 8
                    if with_sink:
                        V.tensor_tensor(row_sum[:, c:c + 1], row_sum[:, c:c + 1], sink_exp[:, c:c + 1], ALU.add)
                        V.drain()
                    V.reciprocal(inv_sum[:, c:c + 1], row_sum[:, c:c + 1]).then_inc(combined, 1)

                def attend(run, s0, m0, pair0, slab0):
                    for t in range(run.n + 2):
                        now = run.steps[t] if t < run.n else None
                        if t >= 2:
                            probs_lo(s0, t - 2, window(run.steps[t - 2][0], run.steps[t - 2][2])[1])

                        def max_of(k):
                            grp, pp, i, j = now
                            width = window(grp, i)[1] * P
                            if grp == "A":
                                biased_max(s0, m0, t, 1, 2 * t + k, width, far[:, S - width:S], 2 * pair0 + (2 * pp + k))
                            elif grp == "B":
                                biased_max(s0, m0, t, 3, t, width, near[:, 2 * P - width:2 * P], 2 * (pair0 + pp) + j,
                                           4 * l + (2 * (pair0 + pp - B0) + j))
                            else:
                                h = 2 * run.parity + j
                                if i:
                                    dve.wait_ge(bias_done, 28 * l + 14 * run.parity + 2 * (i - 1) + j + 1)
                                V.scalar_tensor_tensor(out=probs[:, t % 4, i * P:width], in0=o_out[:, B0 + j, i * P:width],
                                                       scalar=cum_q[:, i * CH + h:i * CH + h + 1], in1=causal[:],
                                                       op0=ALU.add, op1=ALU.add)
                                V.drain()
                                biased_max(s0, m0, t, 3, t, width, probs[:, t % 4, 0:width], 2 * (pair0 + pp) + j)

                        if now:
                            max_of(0)
                        if 1 <= t <= run.n:
                            grp, pp, i, j = run.steps[t - 1]
                            if grp == "A":
                                combine(m0, t - 1, (i + 1) * P)
                            else:
                                invert_sum(m0, t - 1, grp == "B")
                        if now and run.pair_start[t] and not (now[0] == "B" and now[1] == 2):
                            slot = (run.parity + now[1]) % 2
                            part_low(slab0 + (3 * now[1] - 1), v_lo[:, slot], v_hi[:, slot],
                                     ps[1][:].rearrange("p (b d) -> p b d", d=P))
                        if now and now[0] == "A":
                            max_of(1)
                        k = run.ends(t - 1)
                        if k is not None and k % 3 < 2:
                            slot = (run.parity + 1 + k // 3) % 2
                            part_low(slab0 + k, (q_lo, k_lo)[k % 3][:, slot], (q_hi, k_hi)[k % 3][:, slot], part[:])
                        if k is not None:
                            if not (run is RUN_CB and k >= 2):
                                split_proj(slab0 + (k + 2), (run.parity + k) % 2)
                            elif k == 3:
                                split_w(l, 1, 0, 0)
                        k = run.ends(t)
                        if k is not None:
                            evacuate(slab0 + k, pair0 + (1 + k // 3), k % 3, 1)

                with dve.Fori(0, 2) as a:
                    attend(RUN_A, STEPS * l + 16 * a, MAPS * l + 32 * a, 2 * a, 6 * a + 4)
                dve.wait_ge(cum_out, 5 * l + 3)
                attend(RUN_C, STEPS * l + 32, MAPS * l + 64, C0, 16)
                dve.wait_ge(cum_out, 5 * l + 5)
                attend(RUN_CB, STEPS * l + 48, MAPS * l + 80, C0 + 1, 19)

                dve.wait_ge(o_rms, l + 1)
                V.reciprocal(o_inv[:], o_inv[:])
                V.drain()
                o_all = o_out[:].rearrange("p s (b e) -> p s b e", e=P)
                for n in range(NC + 1):
                    if n < NC:
                        if n >= 2:
                            dve.wait_ge(y_turned, NC * l + n - 1)
                        y = turn_in[n % 2].rearrange("p (b e) -> p b e", e=P)
                        if n < AH:
                            V.tensor_tensor(y, o_all[:, n], o_inv[:, n * NQ:(n + 1) * NQ].unsqueeze(2).to_broadcast([P, NQ, P]),
                                            ALU.mult).then_inc(y_ready, 1)
                        elif n < AH + 2:
                            V.tensor_copy(y, o_all[:, n]).then_inc(y_ready, 1)
                        else:
                            g = n - AH - 2
                            yb = turn_in[n % 2].rearrange("p (b s e) -> p s b e", s=2, e=HD)
                            for s in range(2):
                                e = V.tensor_copy(yb[:, s], o_all[:, B0 + s, :, g * HD:(g + 1) * HD])
                            e.then_inc(y_ready, 1)
                    if n:
                        c = MIX_CHUNK[n - 1]
                        dve.wait_ge(mix_hi_done, NC * l + n)
                        V.scalar_tensor_tensor(out=mix_lo[:, c], in0=ps[(n - 1) % 2][:],
                                               scalar=mix_gain[:, bass.ds(NC * l + c, 1)],
                                               in1=mix_hi[:, c].bitcast(F32), op0=ALU.mult,
                                               op1=ALU.subtract).then_inc(mix_split, 1)

                def residual(mm, m, j):
                    r = result(l, 1, mm, j)
                    V.tensor_tensor(xt[:, 2 * m + j], r, xt[:, 2 * m + j], ALU.add).then_inc(evacuated, 1)

                def add_out(m, half):
                    for j in range(2):
                        split_w(l, 1, m + j, 1 - j)
                        dve.wait_ge(x_back[half], 16 * l + 16)
                        residual(m, m, j)
                        dve.wait_ge(h_hi_done, 2 * NC * l + 2 * m + (NC + j + 1))
                        V.scalar_tensor_tensor(out=h_lo[:, 2 * m + j], in0=xt[:, 2 * m + j],
                                               scalar=param[:, bass.ds(2 * NC * l + 2 * m + (NC + j), 1)],
                                               in1=h_hi[:, 2 * m + j].bitcast(F32), op0=ALU.mult,
                                               op1=ALU.subtract).then_inc(h_split, 1)

                for i in range(2):
                    with dve.Fori(NC // 4 * i, NC // 4 * (i + 1)) as m:
                        add_out(m, i)

                def hidden(g, m, j):
                    r = result(l, 1, NC * g + m + NC // 2, j)
                    V.scalar_tensor_tensor(out=ring[j][:], in0=r, scalar=0.0, in1=inv_rms[:], op0=ALU.max,
                                           op1=ALU.mult).then_inc(evacuated, 1)
                    dve.wait_ge(relu_sq, 4 * NC * l + NC * g + 2 * m + (j + 1))
                    V.tensor_tensor(u_lo[:, 2 * m + j], ring[j][:], u_hi[:, 2 * m + j].bitcast(F32),
                                    ALU.subtract).then_inc(u_split, 1)

                split_w(l, 1, NC // 2, 1)
                invert_rms(2 * l + 2)
                hidden(0, 0, 0)
                split_w(l, 1, NC // 2 + 1, 0)
                hidden(0, 0, 1)

                def up(g, m):
                    for j in range(2):
                        split_w(l, 1, NC * g + m + (NC // 2 + j), 1 - j)
                        hidden(g, m, j)

                def down(g, m, last):
                    for j in range(2):
                        if not (last and isinstance(m, int) and j == 1):
                            split_w(l, 1, NC * g + m + (NC + j), 1 - j)
                        residual(NC * g + m + NC, m, j)
                        if last:
                            dve.wait_ge(h_hi_done, 2 * NC * l + 2 * m + (2 * NC + j + 1))
                            V.scalar_tensor_tensor(out=h_lo[:, 2 * m + j], in0=xt[:, 2 * m + j],
                                                   scalar=param[:, bass.ds(2 * NC * l + 2 * m + (2 * NC + j), 1)],
                                                   in1=h_hi[:, 2 * m + j].bitcast(F32), op0=ALU.mult,
                                                   op1=ALU.subtract).then_inc(h_split, 1)

                with dve.Fori(1, NC // 2) as m:
                    up(0, m)
                with dve.Fori(0, NC // 2) as m:
                    down(0, m, False)
                with dve.Fori(1, GROUPS - 1) as g:
                    with dve.Fori(0, NC // 2) as m:
                        up(g, m)
                    with dve.Fori(0, NC // 2) as m:
                        down(g, m, False)
                with dve.Fori(0, NC // 2) as m:
                    up(GROUPS - 1, m)
                with dve.Fori(0, NC // 2 - 1) as m:
                    down(GROUPS - 1, m, True)
                down(GROUPS - 1, NC // 2 - 1, True)

            invert_rms(2 * DEPTH + 1)
            for c in range(NC):
                if c >= 2:
                    dve.wait_ge(y_turned, NC * DEPTH + c - 1)
                V.scalar_tensor_tensor(out=turn_in[c % 2], in0=xt[:, c],
                                       scalar=param[:, 2 * DEPTH * NC + c:2 * DEPTH * NC + c + 1], in1=inv_rms[:],
                                       op0=ALU.mult, op1=ALU.mult).then_inc(y_ready, 1)

        @block.tensor
        def _(pe):
            def products(region, m, j, l, hi, lo, ready, count, order=range(NC)):
                pe.wait_ge(w_split, NSLAB * l + slab_no(region, m, j) + (1 + CREDIT))
                pe.wait_ge(evacuated, NSLAB * l + ring_free(region, m, j))
                pe.wait_ge(ready, count - 1)
                for c in order:
                    if c == order[-1]:
                        pe.wait_ge(ready, count)
                    for n, (w, h) in enumerate(((w_hi, hi), (w_hi, lo), (w_lo, hi))):
                        for t in range(S // BANK):
                            mm = nc.tensor.matmul(ps[j][:, bass.ts(t, BANK)], w[:, j, c], h[:, c, bass.ts(t, BANK)],
                                                  start=(c == order[0] and n == 0), stop=(c == order[-1] and n == 2))
                mm.then_inc(slab_done, 1)

            def turn(src, dst, count, done, size=P, idn=None):
                for b in range(count):
                    tr = nc.tensor.transpose(dst[:, b * P:(b + 1) * P], src[:, b * P:(b + 1) * P], ident[:])
                tr.then_inc(done, 1)

            def sum_squares(n):
                pe.wait_ge(sq_added, NC * n + CREDIT)
                for t in range(S // BANK):
                    mm = nc.tensor.matmul(ps[2][:, bass.ts(t, BANK)], ones[:], sq_sum[:, bass.ts(t, BANK)],
                                          start=True, stop=True)
                mm.then_inc(ss_done, 1)

            pe.sem_inc(slab_done, CREDIT)
            pe.sem_inc(turned, CREDIT)
            pe.wait_ge(setup_pool, 6)
            pe.wait_ge(par_loaded, 16 * (2 * DEPTH + 3))
            nc.tensor.transpose(ps[3][:, 0:64], par_raw[:], ident[0:64, 0:64]).then_inc(setup_pe, 1)
            for c in range(NC):
                if c % 2 == 0:
                    pe.wait_ge(x_loaded[c // 2], 16)
                if c >= 2:
                    pe.wait_ge(x_ready, c - 1)
                for b in range(NQ):
                    tr = nc.tensor.transpose(ps[c % 2][:, b * P:(b + 1) * P], rows[:, b, c * P:(c + 1) * P], ident[:])
                tr.then_inc(x_turned, 1)
            pe.wait_ge(x_ready, NC)

            with pe.Fori(0, DEPTH) as l:
                h_count = 2 * NC * l + NC

                def piece(s, j, p, c):
                    for n, (w, h) in enumerate(((w_hi, h_hi), (w_hi, h_lo), (w_lo, h_hi))):
                        for t in range(S // BANK):
                            mm = nc.tensor.matmul(ps[p][:, bass.ts(t, BANK)], w[:, j, c], h[:, c, bass.ts(t, BANK)],
                                                  start=(c == 0 and n == 0), stop=(c == NC - 1 and n == 2))
                    if c == NC - 1:
                        mm.then_inc(slab_done, 1)

                def project(s):
                    pe.wait_ge(w_split, NSLAB * l + s + (1 + CREDIT))
                    pe.wait_ge(evacuated, NSLAB * l + s - 1 + CREDIT)
                    pe.wait_ge(h_split, h_count)
                    for c in range(NC):
                        piece(s, s % 2, s % 2, c)

                def spread(head, p):
                    pick = ident[96:P, F_ROW + head:F_ROW + head + 1].to_broadcast([32, P])
                    for t in range(S // BANK):
                        mm = nc.tensor.matmul(ps[p][:, bass.ts(t, BANK)], pick, cum[96:P, bass.ts(t, BANK)],
                                              start=True, stop=True)
                    mm.then_inc(cum_ps, 1)

                project(0)
                pe.wait_ge(sq_added, 2 * NC * l + (NC + CREDIT))
                for t in range(S // BANK):
                    mm = nc.tensor.matmul(ps[2][:, bass.ts(t, BANK)], ones[:], sq_sum[:, bass.ts(t, BANK)],
                                          start=True, stop=True)
                mm.then_inc(ss_done, 1)
                project(1)
                project(2)
                pe.wait_ge(cum_ready, l + 1)
                pe.wait_ge(rms_done, 2 * l + 1)
                spread(0, 3)
                for b in range(NQ):
                    tr = nc.tensor.transpose(ps[2][:, b * 32:(b + 1) * 32], cum[96:P, b * P:(b + 1) * P],
                                             ident[96:P, 96:P])
                tr.then_inc(cum_ps, 1)
                project(3)
                pe.wait_ge(cum_out, 5 * l + 2)
                spread(1, 2)

                def scores(m0, n, qs, ks, i, j, k0, width):
                    pe.wait_ge(scores_read, m0 + (n + CREDIT))
                    half = slice(j * HD, (j + 1) * HD)
                    for at in range(0, width, BANK):
                        w = min(BANK, width - at)
                        for p, (q, k) in enumerate(((q_hi, k_hi), (q_hi, k_lo), (q_lo, k_hi))):
                            mm = nc.tensor.matmul(ps[0][:, at:at + w], q[half, qs, i * P:(i + 1) * P],
                                                  k[half, ks, k0 * P + at:k0 * P + at + w],
                                                  start=(p == 0), stop=(p == 2))
                    mm.then_inc(scored, 1)

                def turn_probs(s0, t, slot, blocks, ready, count):
                    pe.wait_ge(ready, count)
                    pe.wait_ge(pt_split, s0 + (t + 1))
                    turn(probs[:, slot], ps[2], blocks, turned)

                def values(s0, t, slot, k0, blocks, e0, e1):
                    pe.wait_ge(pt_split, s0 + (t + 2))
                    pe.wait_ge(o_stored, s0 + (t - 1 + CREDIT))
                    o = ps[3][:, BANK * (t % 2):BANK * (t % 2) + e1 - e0]
                    for b in range(blocks):
                        for p, (a, v) in enumerate(((pt_hi, v_hi), (pt_hi, v_lo), (pt_lo, v_hi))):
                            mm = nc.tensor.matmul(o, a[:, b], v[:, slot, k0 + b, e0:e1],
                                                  start=(b == 0 and p == 0), stop=(b == blocks - 1 and p == 2))
                    mm.then_inc(pv_done, 1)

                def attend(run, s0, m0, slab0):
                    def kv_slot(grp, pp):
                        return (run.parity + (1 if grp == "B" else pp)) % 2

                    def score(t, k):
                        grp, pp, i, j = run.steps[t]
                        k0, blocks = window(grp, i)
                        if run.pair_start[t] and k == 0:
                            pe.wait_ge(split_done, NPART * l + slab0 + (3 if grp == "B" and pp == 2 else 3 * pp - 2))
                        n, m = (2 * t + k, k) if grp == "A" else (t, j)
                        scores(m0, n, (run.parity + pp) % 2, kv_slot(grp, pp), i, m, k0, blocks * P)

                    def dense(pieces):
                        for k, c in pieces:
                            if c == 0:
                                s = slab0 + k
                                pe.wait_ge(w_split, NSLAB * l + s + (1 + CREDIT))
                                pe.wait_ge(evacuated, NSLAB * l + s + CREDIT)
                                if k % 3 == 0:
                                    pe.wait_ge(split_done, NPART * l + (s - 1))
                            piece(slab0 + k, (run.parity + k) % 2, 1, c)

                    for t in range(run.n + 2):
                        now = run.steps[t] if t < run.n else None
                        todo = list(run.pieces[t]) if now else []
                        first = now is not None and run.pair_start[t]
                        if now:
                            score(t, 0)
                        if first and not (now[0] == "B" and now[1] == 2):
                            pe.wait_ge(evacuated, NSLAB * l + slab0 + (3 * now[1] + CREDIT))
                            turn(part, ps[1], NQ, v_turned)
                        if now and now[0] == "A" and not first:
                            dense(todo[:1])
                            todo = todo[1:]
                        if t >= 2:
                            grp, pp, i, j = run.steps[t - 2]
                            k0, blocks = window(grp, i)
                            if run.pair_start[t - 2]:
                                pe.wait_ge(split_done, NPART * l + slab0 + (2 if grp == "B" and pp == 2 else 3 * pp - 1))
                            e0, e1 = (0, P) if j is None else (j * HD, (j + 1) * HD)
                            values(s0, t - 2, kv_slot(grp, pp), k0, blocks, e0, e1)
                        if now and now[0] == "A":
                            score(t, 1)
                        if now and not first:
                            dense(todo[:1])
                            todo = todo[1:]
                        if run is RUN_A and t == 1:
                            pe.wait_ge(cum_out, 5 * l + 3)
                        if 1 <= t <= run.n:
                            grp, pp, i, j = run.steps[t - 1]
                            blocks = window(grp, i)[1]
                            if grp == "A":
                                turn_probs(s0, t - 1, (2 * (t - 1)) % 4, blocks, combined, s0 + t)
                            else:
                                turn_probs(s0, t - 1, (t - 1) % 4, blocks, exp_done, m0 + t)
                        dense(todo)

                with pe.Fori(0, 2) as a:
                    attend(RUN_A, STEPS * l + 16 * a, MAPS * l + 32 * a, 6 * a + 4)
                attend(RUN_C, STEPS * l + 32, MAPS * l + 64, 16)
                spread(2, 0)
                spread(3, 2)
                pe.wait_ge(cum_out, 5 * l + 5)
                attend(RUN_CB, STEPS * l + 48, MAPS * l + 80, 19)

                with pe.Fori(0, NC // 2) as m:
                    for j in range(2):
                        pe.wait_ge(y_ready, NC * l + 2 * m + (j + 1))
                        pe.wait_ge(mix_split, NC * l + 2 * m + (j - 1 + CREDIT))
                        turn(turn_in[j], ps[j], NQ, y_turned)
                with pe.Fori(0, NOUT // 2) as m:
                    for j in range(2):
                        products(1, m, j, l, mix_hi, mix_lo, mix_split, NC * l + (NC + CREDIT), MIX_CHUNK)

                def up(g, m, j):
                    products(1, NC * g + m + NC // 2, j, l, h_hi, h_lo, h_split, h_count + NC)

                def down(g, m, j):
                    products(1, NC * g + m + NC, j, l, u_hi, u_lo, u_split, 4 * NC * l + NC * g + NC)

                up(0, 0, 0)
                pe.wait_ge(sq_added, 2 * NC * l + (2 * NC + CREDIT))
                for t in range(S // BANK):
                    mm = nc.tensor.matmul(ps[2][:, bass.ts(t, BANK)], ones[:], sq_sum[:, bass.ts(t, BANK)],
                                          start=True, stop=True)
                mm.then_inc(ss_done, 1)
                up(0, 0, 1)
                with pe.Fori(1, NC // 2) as m:
                    for j in range(2):
                        up(0, m, j)
                with pe.Fori(0, NC // 2) as m:
                    for j in range(2):
                        down(0, m, j)
                with pe.Fori(1, GROUPS) as g:
                    with pe.Fori(0, NC // 2) as m:
                        for j in range(2):
                            up(g, m, j)
                    with pe.Fori(0, NC // 2) as m:
                        for j in range(2):
                            down(g, m, j)

            sum_squares(2 * DEPTH + 1)
            for c in range(NC):
                pe.wait_ge(y_ready, NC * DEPTH + c + 1)
                if c >= 2:
                    pe.wait_ge(mix_hi_done, NC * DEPTH + c - 1)
                turn(turn_in[c % 2], ps[c % 2], NQ, y_turned)


_INS = ["x", "w_in", "a_lambda", "a_subln", "b_sinks", "c_fbias", "w_out", "g_mix", "g_mlp", "w_up", "w_down", "g_final"]


def kernel(**inputs):
    import concourse.bacc as _bacc
    from concourse.bass_utils import run_bass_kernel_spmd as _run

    nc = _bacc.Bacc("TRN2", target_bir_lowering=False, num_devices=1)
    arrays, args = {}, []
    for name in _INS:
        a = np.ascontiguousarray(inputs[name])
        arrays[f"in_{name}_dram"] = a
        args.append(nc.dram_tensor(f"in_{name}_dram", a.shape, mybir.dt.from_np(a.dtype), kind="ExternalInput").ap())
    shape = inputs["x"].shape
    args.append(nc.dram_tensor("out_0_dram", shape, F32, kind="ExternalOutput").ap())
    hybrid_encoder(nc, *args)
    r = _run(nc, [arrays], core_ids=[0])
    return r.results[0]["out_0_dram"]
```

```python
import math
from contextlib import ExitStack

import numpy as np

import concourse.bass as bass
from concourse import mybir

F32 = mybir.dt.float32
F32R = mybir.dt.float32r
ALU = mybir.AluOpType
ACT = mybir.ActivationFunctionType
AX = mybir.AxisListType

P = 128
BANK = 512
KB = 1024


def hybrid_encoder(nc, x, w_in, a_lambda, a_subln, b_sinks, c_fbias, w_out, g_mix, g_mlp,
                   w_up, w_down, g_final, out):
    _, S, D = x.shape
    DEPTH = w_in.shape[0]
    HD = a_lambda.shape[2]
    AH, BH, CH = 4, b_sinks.shape[1], c_fbias.shape[1]
    F = w_up.shape[2]
    CHUNK = 64
    EPS = 1e-5
    NEG = -1e30
    NC = D // P
    NQ = S // P
    GROUPS = F // D
    assert (S, D, HD, F) == (1024, 1024, 64, 4096) and NC == 8 and NQ == 8

    PAIRS = 8
    SPLIT = 1 + 3 * (PAIRS - 1) + 1
    NPART = SPLIT - 1
    NOUT = NC
    NSLAB = SPLIT + NOUT + GROUPS * 2 * NC
    OFF_AK = AH * 2 * HD
    OFF_AV = 2 * OFF_AK
    OFF_BQ = OFF_AV + AH * 2 * HD
    OFF_BK = OFF_BQ + BH * HD
    OFF_BV = OFF_BK + BH * HD // 2
    OFF_CQ = OFF_BV + BH * HD // 2
    OFF_CK = OFF_CQ + CH * HD
    OFF_CV = OFF_CK + CH * HD
    OFF_CF = OFF_CV + CH * HD
    D_IN = OFF_CF + CH
    assert D_IN == w_in.shape[2]
    F_ROW = P - CH
    C0, B0 = AH, AH + 2
    PROJ_COLS = [D_IN - P]
    for n in range(AH):
        PROJ_COLS += [P * n, OFF_AK + P * n, OFF_AV + P * n]
    for n in range(2):
        PROJ_COLS += [OFF_CQ + P * n, OFF_CK + P * n, OFF_CV + P * n]
    PROJ_COLS += [None, OFF_BK, OFF_BV, None]
    assert len(PROJ_COLS) == SPLIT
    CREDIT = 2

    SLOPE_A = [2.0 ** (-8.0 * (2 * h + 1) / (AH + BH)) for h in range(AH)]
    SLOPE_B = [2.0 ** (-8.0 * (2 * h + 2) / (AH + BH)) for h in range(BH)]
    SLOPES = [(s, s) for s in SLOPE_A] + [(1.0, 1.0)] * 2 + [(SLOPE_B[p], SLOPE_B[2 + p]) for p in range(2)]
    STEPS = 80
    MAPS = 128
    WIDE = 32

    PIECES = {"A": [4, 4, 3, 3, 2, 3, 3, 2], "C": [1] * 4 + [2] * 6 + [1, 2, 1, 2, 1, 1], "B": [2] + [1] * 6 + [0]}
    END_PIECES = {"A": [4, 4, 3, 3, 2, 2, 2, 2, 2], "C": [2] * 7 + [1] * 9 + [1], "B": [0] * 9}

    LATER = {"A": 1, "C": 2, "B": 2}

    class Run:

        def __init__(self, groups, parity):
            self.parity = parity
            self.steps, self.pieces, self.ended = [], [], []
            self.pair_start, self.map0 = [], []
            counts = []
            for pp, grp in enumerate(groups):
                for u in range(2 * NQ if grp == "C" else NQ):
                    self.map0.append(self.map0[-1] + self.maps(-1) if self.steps else 0)
                    self.steps.append((grp, pp, u // 2, u % 2) if grp == "C" else (grp, pp, u, None))
                    self.pair_start.append(u == 0)
                counts += (END_PIECES if pp == len(groups) - 1 else PIECES)[grp]
            at = 0
            for count in counts:
                self.pieces.append([(k // NC, k % NC) for k in range(at, at + count)])
                at += count
                self.ended.append(at // NC - 1 if count and at // NC > (at - count) // NC else None)
            self.n = len(self.steps)
            self.next_pair = None if groups[-1] == "B" else len(groups)

        def maps(self, t):
            return 1 if self.steps[t][0] == "C" else 2

        def ends(self, t):
            return self.ended[t] if 0 <= t < len(self.ended) else None

        def weights_at(self, t):
            if t == self.n + 1 and self.ends(self.n) is not None:
                return self.ends(self.n)
            later = LATER[self.steps[min(t, self.n - 1)][0]]
            return self.ends(t - later) if t - later < self.n else None

        def values_turned(self, t):
            if t < self.n and t > 0 and self.pair_start[t] and self.steps[t][:2] != ("B", 2):
                return self.steps[t][1]
            return self.next_pair if t == self.n + 1 else None

        def early(self, t):
            return t >= 1 and t < self.n and self.steps[t][0] == "B" and self.steps[t - 1][0] == "B"

        def wide(self, w0, t):
            if self.turned_blocks(t) <= NQ // 2:
                return None
            return w0 + sum(self.turned_blocks(u) > NQ // 2 for u in range(t))

        def half(self, t):
            return NQ // 2 * (t % 2) if self.steps[t][0] == "B" else 0

        def turned_blocks(self, t):
            grp, _, i, _ = self.steps[t]
            return window(grp, i)[1] * (2 if grp == "B" else 1)

    FINAL_PS = (0, 1, 3)
    MIX_CHUNK = [0, 1, 2, 3, 6, 7, 4, 5]

    def window(grp, i):
        blocks = min(i + 1, 2) if grp == "B" else i + 1
        return i + 1 - blocks, blocks

    RUN_A, RUN_C, RUN_CB = Run("AA", 0), Run("C", 0), Run("CBB", 1)

    x_rows = x[0].rearrange("(b p) d -> p b d", p=P)
    out_rows = out[0].rearrange("(b p) d -> p b d", p=P)
    x_saved = nc.dram_tensor("x_saved", (P, NC * S), F32, kind="Internal").ap()

    with ExitStack() as ctx:
        def sem(name):
            return ctx.enter_context(nc.semaphore(name))

        base = (nc.sbuf_base + 31) // 32 * 32

        def place(name, shape, offset, dtype=F32):
            return nc.alloc_sbuf_tensor_at(name, shape, dtype, offset=base + offset)

        W_AT, H_AT, PART_AT, PROBS_AT, PT_AT = 0, 20 * KB, 84 * KB, 132 * KB, 148 * KB
        TMP_AT, RMS_AT, GATE_AT, X_AT, T_AT = 156 * KB, 160 * KB, 164 * KB, 168 * KB, 200 * KB
        w_raw = place("w_raw", [P, NC, P], W_AT)
        w_hi = place("w_hi", [P, 2, NC, P], W_AT + 4 * KB, F32R)
        w_lo = place("w_lo", [P, 2, NC, P], W_AT + 12 * KB, F32R)
        h_hi = place("h_hi", [P, NC, S], H_AT, F32R)
        h_lo = place("h_lo", [P, NC, S], H_AT + 32 * KB, F32R)
        q_hi = place("q_hi", [P, 2, S], PART_AT, F32R)
        q_lo = place("q_lo", [P, 2, S], PART_AT + 8 * KB, F32R)
        k_hi = place("k_hi", [P, 2, S], PART_AT + 16 * KB, F32R)
        k_lo = place("k_lo", [P, 2, S], PART_AT + 24 * KB, F32R)
        v_parts = place("v_parts", [P, 2, NQ, 2, P], PART_AT + 32 * KB, F32R)
        probs = place("probs", [P, 4, S], PROBS_AT)
        pt_hi = place("pt_hi", [P, NQ, P], PT_AT, F32R)
        pt_lo = place("pt_lo", [P, NQ, P], PT_AT + 4 * KB, F32R)
        mix_hi = place("mix_hi", [P, NC, S], PART_AT, F32R)
        mix_lo = place("mix_lo", [P, NC, S], PART_AT + 32 * KB, F32R)
        u_hi = place("u_hi", [P, NC, S], PART_AT, F32R)
        u_lo = place("u_lo", [P, NC, S], PART_AT + 32 * KB, F32R)
        rows = place("rows", [P, NQ, D], PART_AT)
        ring = [place("ring0", [P, S], PT_AT), place("ring1", [P, S], PT_AT + 4 * KB)]
        turn_in = [probs[:, 0], probs[:, 1]]
        gate_tmp = place("gate_tmp", [P, S], PT_AT)
        sq_sum = place("sq_sum", [P, S], TMP_AT)
        part = place("part", [P, S], TMP_AT)
        inv_rms = place("inv_rms", [P, S], RMS_AT)
        cum = place("cum", [P, S], GATE_AT)
        lam_raw = place("lam_raw", [P, DEPTH * 4 * HD], GATE_AT)
        lam_prod_place = place("lam_prod", [P, DEPTH * 2 * HD], RMS_AT)
        o_out = place("o_out", [P, PAIRS, S], X_AT)
        xt = place("xt", [P, NC, S], X_AT)
        cursor = [T_AT]

        def small(name, shape, dtype=F32):
            t = place(name, shape, cursor[0], dtype)
            cursor[0] += (4 * int(np.prod(shape[1:])) + 31) // 32 * 32
            assert base + cursor[0] <= nc.sbuf_usable_end
            return t

        ident = small("ident", [P, P])
        ones = small("ones", [P, 1])
        far = small("far", [P, S])
        near = small("near", [P, 2 * P])
        causal = small("causal", [P, P])
        NPAR = (2 * DEPTH + 1) * NC
        param = small("param", [P, 64])
        mix_gain = small("mix_gain", [P, DEPTH * NC])
        q_scale = small("q_scale", [P, PAIRS])
        slope = small("slope", [P, 16])
        neg_slope = small("neg_slope", [P, 16])
        sink_raw = small("sink_raw", [P, DEPTH * BH])
        sink = small("sink", [P, DEPTH * 4])
        neg_lam = small("neg_lam", [P, DEPTH])
        lam_dot = small("lam_dot", [P, DEPTH * 2])
        eps = small("eps", [P, 1])
        rms_col = small("rms_col", [P, NQ])
        row_max = small("row_max", [P, 8])
        neg_max = small("neg_max", [P, 8])
        row_sum = small("row_sum", [P, 8])
        sink_exp = small("sink_exp", [P, 8])
        inv_sum = small("inv_sum", [P, 8])
        lam_ratio = small("lam_ratio", [P, 8])
        o_sq = small("o_sq", [P, AH * NQ])
        o_inv = small("o_inv", [P, AH * NQ])
        o_sq_now = small("o_sq_now", [P, 2 * NQ])
        slope_now = small("slope_now", [P, 4])
        wait_slot = small("wait_slot", [P, 1])
        cum_q = small("cum_q", [P, NQ * CH])
        par_raw = place("par_raw", [64, P], TMP_AT)

        ps = [ctx.enter_context(nc.psum_tensor(f"ps{i}", [P, 2 * BANK], F32)) for i in range(4)]

        w_loaded = sem("w_loaded")
        w_hi_done = sem("w_hi_done")
        w_split = sem("w_split")
        slab_done = sem("slab_done")
        evacuated = sem("evacuated")
        x_loaded = [sem(f"x_loaded{i}") for i in range(4)]
        x_turned = sem("x_turned")
        x_ready = sem("x_ready")
        squared = sem("squared")
        sq_added = sem("sq_added")
        h_hi_done = sem("h_hi_done")
        h_split = sem("h_split")
        ss_done = sem("ss_done")
        rms_done = sem("rms_done")
        rms_inverted = sem("rms_inverted")
        rms_spread = sem("rms_spread")
        rms_out = sem("rms_out")
        rows_done = sem("rows_done")
        relu_sq = sem("relu_sq")
        u_split = sem("u_split")
        part_hi = sem("part_hi")
        split_done = sem("split_done")
        v_turned = sem("v_turned")
        x_spilled = sem("x_spilled")
        x_back = [sem("x_back0"), sem("x_back1")]
        gate_log = sem("gate_log")
        cum_ready = sem("cum_ready")
        cum_ps = sem("cum_ps")
        cum_out = sem("cum_out")
        scored = sem("scored")
        scores_read = sem("scores_read")
        max_done = sem("max_done")
        bias_done = sem("bias_done")
        exp_done = sem("exp_done")
        combined = sem("combined")
        turned = sem("turned")
        first_turned = sem("first_turned")
        first_hi = sem("first_hi")
        first_split = sem("first_split")
        pt_hi_done = sem("pt_hi_done")
        pt_split = sem("pt_split")
        pv_done = sem("pv_done")
        o_summed = sem("o_summed")
        o_stored = sem("o_stored")
        o_inv_done = sem("o_inv_done")
        o_scaled = sem("o_scaled")
        o_rms = sem("o_rms")
        y_ready = sem("y_ready")
        y_turned = sem("y_turned")
        mix_hi_done = sem("mix_hi_done")
        mix_split = sem("mix_split")
        setup_pool = sem("setup_pool")
        setup_dve = sem("setup_dve")
        setup_act = sem("setup_act")
        setup_pe = sem("setup_pe")
        par_loaded = sem("par_loaded")
        bc_loaded = sem("bc_loaded")
        out_done = sem("out_done")

        block = ctx.enter_context(nc.Block())

        def w_dram(matrix, l):
            return matrix[l].rearrange("(c p) n -> p c n", p=P)

        def slab_no(region, m, j):
            return 2 * m + j + (SPLIT if region else 0)

        def ring_free(region, m, j):
            if region and isinstance(m, int) and m == 0:
                return SPLIT + CREDIT
            return slab_no(region, m, j) - 1 + CREDIT

        @block.sync
        def _(sp):
            def load_x(i):
                w = D // 4
                sp.dma_start(rows[:, :, i * w:(i + 1) * w], x_rows[:, :, i * w:(i + 1) * w]).then_inc(x_loaded[i], 16)

            load_x(0)
            sp.wait_ge(setup_pool, 1)
            r = 0
            for l in range(DEPTH):
                for g in (g_mix, g_mlp):
                    sp.dma_start(par_raw[r:r + NC, :], g[l].rearrange("(c p) -> c p", p=P)).then_inc(par_loaded, 16)
                    r += NC
            sp.dma_start(par_raw[r:r + NC, :], g_final.rearrange("(c p) -> c p", p=P)).then_inc(par_loaded, 16)
            sp.dma_start(par_raw[NPAR:NPAR + DEPTH, :], a_subln).then_inc(par_loaded, 16)
            sp.dma_start(par_raw[NPAR + DEPTH:NPAR + 2 * DEPTH, F_ROW:P], c_fbias).then_inc(par_loaded, 16)
            sp.dma_start(lam_raw[:], a_lambda.rearrange("(o l) k d -> o (l k d)", o=1).to_broadcast([P, DEPTH * 4 * HD])).then_inc(bc_loaded, 16)
            sp.dma_start(sink_raw[:], b_sinks.rearrange("(o l) h -> o (l h)", o=1).to_broadcast([P, DEPTH * BH])).then_inc(bc_loaded, 16)
            for i in range(1, 4):
                load_x(i)

            def load(l, s, parts):
                sp.wait_ge(w_split, NSLAB * l + s + CREDIT)
                for dst, src in parts:
                    sp.dma_start(dst, src).then_inc(w_loaded, 16)

            def halves(src):
                h = NC // 2
                return [(w_raw[:, h:NC], src[:, h:NC]), (w_raw[:, 0:h], src[:, 0:h])]

            with sp.Fori(0, DEPTH) as l:
                win = w_dram(w_in, l)

                def load_proj(s):
                    c0 = PROJ_COLS[s]
                    if c0 is None:
                        at = OFF_BQ + (HD if s == SPLIT - 1 else 0)
                        parts = [(w_raw[:, :, g * HD:(g + 1) * HD],
                                  win[:, :, at + 2 * HD * g:at + 2 * HD * g + HD]) for g in range(2)]
                    else:
                        parts = halves(win[:, :, c0:c0 + P])
                    load(l, s, parts)

                for s in range(2):
                    load_proj(s)
                sp.wait_ge(h_split, 2 * NC * l + NC)
                sp.dma_start(x_saved, xt[:].rearrange("p c s -> p (c s)")).then_inc(x_spilled, 16)
                for s in range(2, SPLIT):
                    load_proj(s)
                wo = w_dram(w_out, l).rearrange("p c (m j n) -> m j p c n", j=2, n=P)
                for j in range(2):
                    load(l, SPLIT + j, halves(wo[0, j]))
                half = NC // 2
                for i in range(2):
                    sp.wait_ge(y_turned, NC * l + half * (i + 1))
                    sp.dma_start(xt[:, half * i:half * (i + 1)].rearrange("p c s -> p (c s)"),
                                 x_saved[:, half * S * i:half * S * (i + 1)]).then_inc(x_back[i], 16)
                with sp.Fori(1, NOUT // 2) as m:
                    for j in range(2):
                        load(l, slab_no(1, m, j), halves(wo[m, j]))
                up = w_dram(w_up, l).rearrange("p c (g m j n) -> g m j p c n", g=GROUPS, j=2, n=P)
                down = w_down[l].rearrange("(g c p) (m j n) -> g m j p c n", p=P, c=NC, j=2, n=P)
                with sp.Fori(0, GROUPS) as g:
                    with sp.Fori(0, NC // 2) as m:
                        for j in range(2):
                            load(l, slab_no(1, NC * g + (m + NC // 2), j), halves(up[g, m, j]))
                    with sp.Fori(0, NC // 2) as m:
                        for j in range(2):
                            load(l, slab_no(1, NC * g + (m + NC), j), halves(down[g, m, j]))
            for i in range(4):
                w = D // 4
                sp.wait_ge(rows_done, 2 * (i + 1))
                sp.dma_start(out_rows[:, :, i * w:(i + 1) * w], rows[:, :, i * w:(i + 1) * w]).then_inc(out_done, 16)
            sp.wait_ge(out_done, 4 * 16)

        @block.gpsimd
        def _(pool):
            pool.memset(par_raw[:], 0.0).then_inc(setup_pool, 1)
            pool.memset(ident[:], 0.0).then_inc(setup_pool, 1)
            pool.memset(causal[:], 0.0).then_inc(setup_pool, 1)
            pool.iota(far[:], [[-1, S]], base=S - P, channel_multiplier=1,
                      allow_small_or_imprecise_dtypes=True).then_inc(setup_pool, 1)
            pool.iota(near[:], [[-1, 2 * P]], base=P, channel_multiplier=1,
                      allow_small_or_imprecise_dtypes=True).then_inc(setup_pool, 1)
            pool.wait_ge(setup_pool, 5)
            pool.affine_select(out=ident[:], in_=ident[:], compare_op=ALU.not_equal, fill=1.0, base=0,
                               pattern=[[-1, P]], channel_multiplier=1).then_inc(setup_pool, 1)
            pool.affine_select(out=causal[:], in_=causal[:], compare_op=ALU.is_ge, fill=NEG, base=0,
                               pattern=[[-1, P]], channel_multiplier=1).then_inc(setup_pool, 1)
            def add_squares(n0, c, slot):
                pool.wait_ge(squared, n0 + (c + 1))
                if isinstance(c, int) and c == 0:
                    nc.gpsimd.tensor_tensor(sq_sum[:], ring[slot][:], ones[:, 0:1].to_broadcast([P, S]),
                                            ALU.mult).then_inc(sq_added, 1)
                else:
                    pool.wait_ge(sq_added, n0 + (c + CREDIT))
                    nc.gpsimd.tensor_tensor(sq_sum[:], sq_sum[:], ring[slot][:], ALU.add).then_inc(sq_added, 1)

            def norm_squares(n0):
                for c in range(NC):
                    add_squares(n0, c, c % 2)

            pool.sem_inc(sq_added, CREDIT)
            norm_squares(0)
            with pool.Fori(0, DEPTH) as l:
                pool.wait_ge(o_inv_done, l + 1)
                for n in range(AH):
                    o = o_out[:, n].rearrange("p (b e) -> p b e", e=P)
                    nc.gpsimd.tensor_tensor(o, o, o_inv[:, n * NQ:(n + 1) * NQ].unsqueeze(2).to_broadcast([P, NQ, P]),
                                            ALU.mult).then_inc(o_scaled, 1)
                norm_squares(2 * NC * l + NC)
                norm_squares(2 * NC * l + 2 * NC)

        @block.scalar
        def _(act):
            def split_w(l, region, m, j):
                act.wait_ge(w_loaded, 32 * NSLAB * l + 32 * slab_no(region, m, j) + 32)
                act.wait_ge(slab_done, NSLAB * l + ring_free(region, m, j))
                nc.scalar.activation(w_hi[:, j], w_raw[:], ACT.Copy).then_inc(w_hi_done, 1)

            def prepare(n0, gain, c, slot):
                act.wait_ge(sq_added, n0 + c + 1)
                nc.scalar.activation(ring[slot][:], xt[:, c], ACT.Square).then_inc(squared, 1)
                nc.scalar.activation(h_hi[:, c], xt[:, c], ACT.Copy,
                                     scale=param[:, bass.ds(gain, 1)]).then_inc(h_hi_done, 1)

            def root_mean_square(n):
                act.wait_ge(ss_done, n)
                nc.scalar.activation(rms_col[:], ps[2][:, 0:NQ], ACT.Sqrt, bias=eps[:, 0:1], scale=1.0 / D)\
                    .then_inc(rms_done, 1)

            def rms_to_rows(n):
                act.wait_ge(rms_spread, n)
                nc.scalar.activation(inv_rms[:], ps[2][:], ACT.Copy).then_inc(rms_out, 1)

            act.sem_inc(o_stored, CREDIT)
            act.wait_ge(setup_dve, 1)
            nc.scalar.activation(lam_dot[:], lam_dot[:], ACT.Exp).then_inc(setup_act, 1)
            for c in range(NC - 1):
                act.wait_ge(x_ready, c + 1)
                prepare(0, c, c, c % 2)

            with act.Fori(0, DEPTH) as l:
                def split_proj(s, j):
                    act.wait_ge(w_loaded, 32 * NSLAB * l + 32 * s + 32)
                    act.wait_ge(slab_done, NSLAB * l + s - 1 + CREDIT)
                    nc.scalar.activation(w_hi[:, j], w_raw[:], ACT.Copy).then_inc(w_hi_done, 1)

                def part_high(s, dst):
                    act.wait_ge(evacuated, NSLAB * l + s + (1 + CREDIT))
                    nc.scalar.activation(dst, part[:], ACT.Copy).then_inc(part_hi, 1)

                split_proj(0, 0)
                act.wait_ge(x_ready, NC)
                act.wait_ge(evacuated, NSLAB * l + CREDIT)
                prepare(2 * NC * l, 2 * NC * l + NC - 1, NC - 1, 1)
                split_proj(1, 1)
                root_mean_square(2 * l + 1)
                split_proj(2, 0)
                rms_to_rows(2 * l + 1)
                act.wait_ge(evacuated, NSLAB * l + (1 + CREDIT))
                g_in, g_tmp = cum[96:P], gate_tmp[96:P]
                bias = param[96:P, bass.ds(l + (NPAR + DEPTH), 1)]
                nc.scalar.activation(g_tmp, g_in, ACT.Abs, bias=bias)
                act.drain()
                nc.scalar.activation(g_tmp, g_tmp, ACT.Exp, scale=-1.0)
                act.drain()
                nc.scalar.activation(g_tmp, g_tmp, ACT.Ln, bias=1.0).then_inc(gate_log, 1)
                split_proj(3, 1)
                part_high(1, q_hi[:, 0])
                split_proj(4, 0)
                part_high(2, k_hi[:, 0])

                def spread_out(head, n, p):
                    act.wait_ge(cum_ps, 5 * l + n)
                    nc.scalar.activation(o_out[:, B0 + head % 2], ps[p][:], ACT.Copy, scale=-1.0).then_inc(cum_out, 1)

                act.wait_ge(x_spilled, 16 * l + 16)
                spread_out(0, 1, 3)
                act.wait_ge(cum_ps, 5 * l + 2)
                nc.scalar.activation(cum_q[:].rearrange("p (b h) -> p b h", h=CH),
                                     ps[2][:, 0:NQ * 32].rearrange("p (b h) -> p b h", h=32)[:, :, 32 - CH:32],
                                     ACT.Copy).then_inc(cum_out, 1)
                split_proj(5, 1)
                spread_out(1, 3, 2)

                def values_high(pair, slot):
                    act.wait_ge(v_turned, (PAIRS - 1) * l + pair + 1)
                    nc.scalar.activation(v_parts[:, slot, :, 0], ps[1][:].rearrange("p (b d) -> p b d", d=P),
                                         ACT.Copy).then_inc(part_hi, 1)

                values_high(0, 0)

                def forget_bias(t, run, s0):
                    grp, pp, i, j = run.steps[t]
                    if grp != "C" or i == 0:
                        return
                    if t >= 4:
                        act.wait_ge(turned, s0 + (t - 3 + CREDIT))
                    h = 2 * run.parity + j
                    nc.scalar.activation(probs[:, t % 4, 0:i * P], o_out[:, B0 + j, 0:i * P], ACT.Identity,
                                         bias=cum_q[:, i * CH + h:i * CH + h + 1]).then_inc(bias_done, 1)

                def probs_hi(s0, t, b0, blocks, wide):
                    if wide is not None:
                        act.wait_ge(first_turned, WIDE * l + wide + 1)
                        nc.scalar.activation(pt_hi[:, 0:NQ // 2], ps[2][:, 0:BANK].rearrange("p (b q) -> p b q", q=P),
                                             ACT.Copy).then_inc(first_hi, 1)
                        b0, blocks = NQ // 2, blocks - NQ // 2
                    act.wait_ge(turned, s0 + (t + 1 + CREDIT))
                    nc.scalar.activation(pt_hi[:, b0:b0 + blocks],
                                         ps[2][:, b0 * P:(b0 + blocks) * P].rearrange("p (b q) -> p b q", q=P),
                                         ACT.Copy).then_inc(pt_hi_done, 1)

                def store_o(s0, t, pair, grp, i, j, n):
                    act.wait_ge(o_summed, s0 + (t + 1))
                    sums = BANK * (t % 2) + 2 * P
                    if grp == "B":
                        for k in range(2):
                            at = i * P + (pair - B0) * HD
                            e = nc.scalar.activation(o_out[:, B0 + k, at:at + HD],
                                                     ps[3][:, sums + k * HD:sums + (k + 1) * HD],
                                                     ACT.Copy, scale=inv_sum[:, (n + k) % 8:(n + k) % 8 + 1])
                        e.then_inc(o_stored, 1)
                        return
                    w = P if j is None else HD
                    at = i * P + (0 if j is None else HD * j)
                    o = ps[3][:, sums:sums + w]
                    inv = inv_sum[:, n % 8:n % 8 + 1]
                    if j is None:
                        nc.scalar.activation(ps[3][:, sums + P:sums + 2 * P], o, ACT.Square, scale=inv,
                                             accum_out=o_sq_now[:, t:t + 1])
                    nc.scalar.activation(o_out[:, pair, at:at + w], o, ACT.Copy, scale=inv).then_inc(o_stored, 1)

                def exponentials(m0, n, width, sl, sink_at=None):
                    act.wait_ge(max_done, m0 + (n + 1))
                    e = nc.scalar.activation(probs[:, n % 4, 0:width], probs[:, n % 4, 0:width], ACT.Exp,
                                             bias=neg_max[:, n % 8:n % 8 + 1], scale=sl,
                                             accum_out=row_sum[:, n % 8:n % 8 + 1])
                    if sink_at is not None:
                        e = nc.scalar.activation(sink_exp[:, n % 8:n % 8 + 1], sink[:, bass.ds(sink_at, 1)], ACT.Exp,
                                                 bias=neg_max[:, n % 8:n % 8 + 1], scale=sl)
                    e.then_inc(exp_done, 1)

                def attend(run, s0, m0, w0, pair0, slab0):
                    if run is RUN_C or run is RUN_CB:
                        forget_bias(0, run, s0)
                    for t in range(run.n + 2):
                        now = run.steps[t] if t < run.n else None
                        if t >= 2:
                            probs_hi(s0, t - 2, run.half(t - 2), run.turned_blocks(t - 2), run.wide(w0, t - 2))
                        if t + 1 < run.n:
                            forget_bias(t + 1, run, s0)

                        def exp_of(k):
                            grp, pp, i, j = now
                            width = window(grp, i)[1] * P
                            n = run.map0[t] + k
                            if grp == "A":
                                exponentials(m0, n, width, slope_now[:, 2 * pp + k:2 * pp + k + 1])
                            else:
                                at = 2 * (pair0 + pp) + k + (j or 0)
                                exponentials(m0, n, width, slope[:, at:at + 1],
                                             4 * l + (at - 2 * B0) if grp == "B" else None)

                        if now:
                            exp_of(0)
                        pp = run.values_turned(t)
                        if pp is not None:
                            values_high(pair0 + pp, (run.parity + pp) % 2)
                        k = run.ends(t - 1)
                        if k is not None and k % 3 < 2:
                            slot = (run.parity + 1 + k // 3) % 2
                            part_high(slab0 + k, (q_hi, k_hi)[k % 3][:, slot])
                        if now and now[0] == "B":
                            exp_of(1)
                        if t >= 2:
                            grp, pp, i, j = run.steps[t - 2]
                            store_o(s0, t - 2, pair0 + pp, grp, i, j, run.map0[t - 2])
                        if now and now[0] == "A":
                            exp_of(1)
                        k = run.weights_at(t)
                        if k is not None:
                            if not (run is RUN_CB and k >= 2):
                                split_proj(slab0 + (k + 2), (run.parity + k) % 2)
                            elif k == 3:
                                split_w(l, 1, 0, 0)

                with act.Fori(0, 2) as a:
                    nc.scalar.activation(slope_now[:], slope[:, bass.ds(4 * a, 4)], ACT.Copy)
                    act.drain()
                    attend(RUN_A, STEPS * l + 16 * a, MAPS * l + 32 * a, 8 * a, 2 * a, 6 * a + 4)
                    act.drain()
                    nc.scalar.activation(o_sq[:, bass.ts(a, 2 * NQ)], o_sq_now[:], ACT.Copy)
                act.drain()
                nc.scalar.activation(o_inv[:], o_sq[:], ACT.Sqrt, bias=eps[:, 0:1], scale=1.0 / P).then_inc(o_rms, 1)
                attend(RUN_C, STEPS * l + 32, MAPS * l + 64, 16, C0, 16)
                act.drain()
                spread_out(2, 4, 0)
                spread_out(3, 5, 2)
                act.drain()
                attend(RUN_CB, STEPS * l + 48, MAPS * l + 80, 24, C0 + 1, 19)

                for n, c in enumerate(MIX_CHUNK):
                    act.wait_ge(y_turned, NC * l + n + 1)
                    nc.scalar.activation(mix_hi[:, c], ps[2 + n % 2][:], ACT.Copy,
                                         scale=mix_gain[:, bass.ds(NC * l + c, 1)]).then_inc(mix_hi_done, 1)

                def prepared(n0, gain, m_slab, m, j, n_slab):
                    act.wait_ge(evacuated, NSLAB * l + n_slab + (1 + CREDIT))
                    prepare(n0, gain, 2 * m + j, j)

                with act.Fori(0, NOUT // 2) as m:
                    for j in range(2):
                        split_w(l, 1, m + j, 1 - j)
                        prepared(2 * NC * l + NC, 2 * NC * l + NC + 2 * m + j, m, m, j, slab_no(1, m, j))

                def hidden(g, m, j):
                    act.wait_ge(evacuated, NSLAB * l + slab_no(1, NC * g + m + NC // 2, j) + (1 + CREDIT))
                    nc.scalar.activation(ring[j][:], ring[j][:], ACT.Square)
                    act.drain()
                    nc.scalar.activation(u_hi[:, 2 * m + j], ring[j][:], ACT.Copy).then_inc(relu_sq, 1)

                split_w(l, 1, NC // 2, 1)
                root_mean_square(2 * l + 2)
                split_w(l, 1, NC // 2 + 1, 0)
                rms_to_rows(2 * l + 2)
                hidden(0, 0, 0)
                hidden(0, 0, 1)

                def up(g, m):
                    for j in range(2):
                        split_w(l, 1, NC * g + m + (NC // 2 + j), 1 - j)
                        hidden(g, m, j)

                def down(g, m, last):
                    for j in range(2):
                        if not (last and isinstance(m, int) and j == 1):
                            split_w(l, 1, NC * g + m + (NC + j), 1 - j)
                        if last and not (isinstance(m, int) and j == 1):
                            prepared(2 * NC * l + 2 * NC, 2 * NC * l + 2 * NC + 2 * m + j, m, m, j,
                                     slab_no(1, NC * g + m + NC, j))

                with act.Fori(1, NC // 2) as m:
                    up(0, m)
                with act.Fori(0, NC // 2) as m:
                    down(0, m, False)
                with act.Fori(1, GROUPS - 1) as g:
                    with act.Fori(0, NC // 2) as m:
                        up(g, m)
                    with act.Fori(0, NC // 2) as m:
                        down(g, m, False)
                with act.Fori(0, NC // 2) as m:
                    up(GROUPS - 1, m)
                with act.Fori(0, NC // 2 - 1) as m:
                    down(GROUPS - 1, m, True)
                down(GROUPS - 1, NC // 2 - 1, True)

            for c in range(NC):
                if c == 0:
                    act.wait_ge(evacuated, NSLAB * DEPTH + CREDIT)
                    act.wait_ge(sq_added, 2 * NC * DEPTH + NC)
                    nc.scalar.activation(ring[1][:], xt[:, NC - 1], ACT.Square).then_inc(squared, 1)
                if c == 4:
                    root_mean_square(2 * DEPTH + 1)
                if c >= 2:
                    act.wait_ge(y_turned, NC * DEPTH + c - 1)
                nc.scalar.activation(turn_in[c % 2], xt[:, c], ACT.Copy,
                                     scale=param[:, 2 * DEPTH * NC + c:2 * DEPTH * NC + c + 1]).then_inc(y_ready, 1)

        @block.vector
        def _(dve):
            V = nc.vector

            V.memset(ones[:], 1.0)
            V.memset(eps[:], EPS)
            for q, (s_lo, s_hi) in enumerate(SLOPES):
                for j, s in enumerate((s_lo, s_hi)):
                    V.memset(slope[:, 2 * q + j:2 * q + j + 1], s)
                    V.memset(neg_slope[:, 2 * q + j:2 * q + j + 1], -s)
                    V.memset(q_scale[j * HD:(j + 1) * HD, q:q + 1], HD ** -0.5 / s)
            V.memset(mix_gain[:], 1.0)
            dve.wait_ge(setup_pool, 5)
            for t in (far, near):
                V.scalar_tensor_tensor(out=t[:], in0=t[:], scalar=-1.0, in1=t[:], op0=ALU.mult, op1=ALU.min)
            V.drain()
            for t, w in ((far, S), (near, 2 * P)):
                V.memset(t[0:CHUNK, w - CHUNK:w], NEG)
            V.memset(near[:, 0:CHUNK], NEG)
            V.memset(near[CHUNK:P, CHUNK:P], NEG)
            dve.wait_ge(bc_loaded, 32)
            lam4 = lam_raw[:].rearrange("p (a k d) -> p a k d", k=2, d=HD)
            lam_prod = lam_prod_place[:].rearrange("p (a d) -> p a d", d=HD)
            V.tensor_tensor(lam_prod, lam4[:, :, 0], lam4[:, :, 1], ALU.mult)
            V.drain()
            V.tensor_reduce(lam_dot[:], lam_prod, AX.X, ALU.add).then_inc(setup_dve, 1)
            for l in range(DEPTH):
                for p in range(2):
                    for j in range(2):
                        at = 4 * l + 2 * p + j
                        h = 2 * j + p
                        V.tensor_scalar(sink[:, at:at + 1], sink_raw[:, l * BH + h:l * BH + h + 1], 1.0 / SLOPE_B[h],
                                        None, ALU.mult)
            dve.wait_ge(setup_act, 1)
            for l in range(DEPTH):
                lam_init = 0.8 - 0.6 * math.exp(-0.3 * l)
                V.tensor_tensor(neg_lam[:, l:l + 1], lam_dot[:, 2 * l + 1:2 * l + 2], lam_dot[:, 2 * l:2 * l + 1],
                                ALU.subtract)
                V.drain()
                V.tensor_scalar(neg_lam[:, l:l + 1], neg_lam[:, l:l + 1], -lam_init, None, ALU.add)
            dve.wait_ge(setup_pe, 1)
            V.tensor_copy(param[:], ps[3][:, 0:64])
            V.drain()
            for l in range(DEPTH):
                lam_init = 0.8 - 0.6 * math.exp(-0.3 * l)
                for c in range(AH):
                    V.tensor_scalar(mix_gain[:, l * NC + c:l * NC + c + 1], param[:, NPAR + l:NPAR + l + 1],
                                    1.0 - lam_init, None, ALU.mult)
            V.drain()
            dve.sem_inc(w_split, CREDIT)
            dve.sem_inc(evacuated, CREDIT)
            dve.sem_inc(scores_read, CREDIT)
            dve.sem_inc(pt_split, 1)
            dve.sem_inc(mix_split, CREDIT)

            def split_w(l, region, m, j):
                dve.wait_ge(w_hi_done, NSLAB * l + slab_no(region, m, j) + 1)
                V.tensor_tensor(w_lo[:, j], w_raw[:], w_hi[:, j].bitcast(F32), ALU.subtract).then_inc(w_split, 1)

            def result(l, region, m, j):
                dve.wait_ge(slab_done, NSLAB * l + slab_no(region, m, j) + (1 + CREDIT))
                return ps[j][:]

            def h_low(n0, gain, c):
                dve.wait_ge(h_hi_done, n0 + c + 1)
                V.scalar_tensor_tensor(out=h_lo[:, c], in0=xt[:, c], scalar=param[:, bass.ds(gain, 1)],
                                       in1=h_hi[:, c].bitcast(F32), op0=ALU.mult, op1=ALU.subtract).then_inc(h_split, 1)

            def invert_rms(n):
                dve.wait_ge(rms_done, n)
                V.reciprocal(rms_col[:], rms_col[:]).then_inc(rms_inverted, 1)

            for c in range(NC):
                dve.wait_ge(x_turned, c + 1)
                V.tensor_copy(xt[:, c], ps[c % 2][:]).then_inc(x_ready, 1)
                if c:
                    h_low(0, c - 1, c - 1)

            with dve.Fori(0, DEPTH) as l:
                def split_proj(s, j):
                    dve.wait_ge(w_hi_done, NSLAB * l + s + 1)
                    V.tensor_tensor(w_lo[:, j], w_raw[:], w_hi[:, j].bitcast(F32), ALU.subtract).then_inc(w_split, 1)

                def part_low(s, lo, hi, src):
                    dve.wait_ge(part_hi, NPART * l + s)
                    V.tensor_tensor(lo, src, hi.bitcast(F32), ALU.subtract).then_inc(split_done, 1)

                def evacuate(s, pair, kind, p):
                    dve.wait_ge(slab_done, NSLAB * l + s + (1 + CREDIT))
                    if kind:
                        dve.wait_ge(split_done, NPART * l + (s - 1))
                    if kind == 0:
                        e = V.scalar_tensor_tensor(out=part[:], in0=ps[p][:], scalar=q_scale[:, bass.ds(pair, 1)],
                                                   in1=inv_rms[:], op0=ALU.mult, op1=ALU.mult)
                    else:
                        e = V.tensor_tensor(part[:], ps[p][:], inv_rms[:], ALU.mult)
                    e.then_inc(evacuated, 1)

                def values_low(s, slot):
                    part_low(s, v_parts[:, slot, :, 1], v_parts[:, slot, :, 0], ps[1][:].rearrange("p (b d) -> p b d", d=P))

                split_proj(0, 0)
                h_low(2 * NC * l, 2 * NC * l + NC - 1, NC - 1)
                split_proj(1, 1)
                invert_rms(2 * l + 1)
                split_proj(2, 0)
                dve.wait_ge(rms_out, 2 * l + 1)
                dve.wait_ge(slab_done, NSLAB * l + 1 + CREDIT)
                V.tensor_tensor(cum[96:P], ps[0][96:P], inv_rms[96:P], ALU.mult).then_inc(evacuated, 1)
                dve.wait_ge(gate_log, l + 1)
                g_in, g_tmp = cum[96:P], gate_tmp[96:P]
                V.tensor_scalar(g_in, g_in, param[96:P, bass.ds(l + (NPAR + DEPTH), 1)], 0.0, ALU.add, ALU.min)
                V.drain()
                V.tensor_tensor(g_tmp, g_in, g_tmp, ALU.subtract)
                V.drain()
                V.tensor_tensor_scan(g_in, ones[96:P, 0:1].to_broadcast([32, S]), g_tmp, 0.0, ALU.mult, ALU.add)\
                    .then_inc(cum_ready, 1)
                evacuate(1, 0, 0, 1)
                split_proj(3, 1)
                part_low(1, q_lo[:, 0], q_hi[:, 0], part[:])
                evacuate(2, 0, 1, 0)
                split_proj(4, 0)
                part_low(2, k_lo[:, 0], k_hi[:, 0], part[:])
                evacuate(3, 0, 2, 1)
                split_proj(5, 1)
                values_low(3, 0)

                def probs_lo(s0, t, b0, blocks, wide):
                    if wide is not None:
                        dve.wait_ge(first_hi, WIDE * l + wide + 1)
                        V.tensor_tensor(pt_lo[:, 0:NQ // 2], ps[2][:, 0:BANK].rearrange("p (b q) -> p b q", q=P),
                                        pt_hi[:, 0:NQ // 2].bitcast(F32), ALU.subtract).then_inc(first_split, 1)
                        b0, blocks = NQ // 2, blocks - NQ // 2
                    dve.wait_ge(pt_hi_done, s0 + (t + 1))
                    V.tensor_tensor(pt_lo[:, b0:b0 + blocks],
                                    ps[2][:, b0 * P:(b0 + blocks) * P].rearrange("p (b q) -> p b q", q=P),
                                    pt_hi[:, b0:b0 + blocks].bitcast(F32), ALU.subtract).then_inc(pt_split, 1)

                def biased_max(s0, m0, t, back, n, width, bias, sc, sink_at=None, p0=0):
                    dve.wait_ge(scored, m0 + (n + 1))
                    dve.wait_ge(turned, s0 + (t - back + CREDIT))
                    V.memset(wait_slot[:], 0.0)
                    at = n % 8
                    V.tensor_tensor_reduce(out=probs[:, n % 4, 0:width], in0=ps[0][:, p0:p0 + width], in1=bias, scale=1.0,
                                           scalar=-3e38, op0=ALU.add, op1=ALU.max, accum_out=row_max[:, at:at + 1])\
                        .then_inc(scores_read, 1)
                    V.drain()
                    neg = neg_slope[:, bass.ds(sc, 1)]
                    if sink_at is None:
                        e = V.tensor_scalar(neg_max[:, at:at + 1], row_max[:, at:at + 1], neg, None, ALU.mult)
                    else:
                        e = V.tensor_scalar(neg_max[:, at:at + 1], row_max[:, at:at + 1],
                                            sink[:, bass.ds(sink_at, 1)], neg, ALU.max, ALU.mult)
                    e.then_inc(max_done, 1)

                def combine(m0, n, width):
                    dve.wait_ge(exp_done, m0 + (n + 2))
                    c, s = n % 8, n % 4
                    V.reciprocal(inv_sum[:, c:c + 2], row_sum[:, c:c + 2])
                    V.drain()
                    V.tensor_scalar(lam_ratio[:, c:c + 1], inv_sum[:, c + 1:c + 2], row_sum[:, c:c + 1],
                                    neg_lam[:, bass.ds(l, 1)], ALU.mult, ALU.mult)
                    V.drain()
                    V.scalar_tensor_tensor(out=probs[:, s, 0:width], in0=probs[:, s + 1, 0:width],
                                           scalar=lam_ratio[:, c:c + 1], in1=probs[:, s, 0:width],
                                           op0=ALU.mult, op1=ALU.add).then_inc(combined, 1)

                def invert_sum(m0, n, maps, with_sink):
                    dve.wait_ge(exp_done, m0 + (n + maps))
                    c = slice(n % 8, n % 8 + maps)
                    if with_sink:
                        V.tensor_tensor(row_sum[:, c], row_sum[:, c], sink_exp[:, c], ALU.add)
                        V.drain()
                    V.reciprocal(inv_sum[:, c], row_sum[:, c]).then_inc(combined, 1)

                def sum_values(s0, t, grp):
                    dve.wait_ge(pv_done, s0 + (t + 1))
                    maps, w = (2 if grp == "B" else 1), (P if grp == "A" else HD)
                    at = BANK * (t % 2)
                    both = ps[3][:, at:at + 2 * maps * w].rearrange("p (m h e) -> p m e h", h=2, e=w)
                    V.tensor_reduce(ps[3][:, at + 2 * P:at + 2 * P + maps * w].rearrange("p (m e) -> p m e", e=w),
                                    both, AX.X, ALU.add).then_inc(o_summed, 1)

                def attend(run, s0, m0, w0, pair0, slab0):
                    for t in range(run.n + 2):
                        now = run.steps[t] if t < run.n else None
                        if t >= 2:
                            probs_lo(s0, t - 2, run.half(t - 2), run.turned_blocks(t - 2), run.wide(w0, t - 2))

                        def max_of(k):
                            grp, pp, i, j = now
                            width = window(grp, i)[1] * P
                            n = run.map0[t] + k
                            if grp == "A":
                                biased_max(s0, m0, t, 1, n, width, far[:, S - width:S], 2 * pair0 + (2 * pp + k))
                            elif grp == "B":
                                at = 2 * (pair0 + pp) + k
                                biased_max(s0, m0, t, 1, n, width, near[:, 2 * P - width:2 * P], at,
                                           4 * l + (at - 2 * B0), BANK * k)
                            else:
                                h = 2 * run.parity + j
                                if i:
                                    dve.wait_ge(bias_done, 28 * l + 14 * run.parity + 2 * (i - 1) + j + 1)
                                V.scalar_tensor_tensor(out=probs[:, t % 4, i * P:width], in0=o_out[:, B0 + j, i * P:width],
                                                       scalar=cum_q[:, i * CH + h:i * CH + h + 1], in1=causal[:],
                                                       op0=ALU.add, op1=ALU.add)
                                V.drain()
                                biased_max(s0, m0, t, 3, n, width, probs[:, t % 4, 0:width], 2 * (pair0 + pp) + j)

                        if now:
                            max_of(0)
                        if 1 <= t <= run.n:
                            grp, pp, i, j = run.steps[t - 1]
                            if grp == "A":
                                combine(m0, run.map0[t - 1], (i + 1) * P)
                            else:
                                invert_sum(m0, run.map0[t - 1], run.maps(t - 1), grp == "B")
                        if now and now[0] == "B":
                            max_of(1)
                        if t >= 2:
                            sum_values(s0, t - 2, run.steps[t - 2][0])
                        pp = run.values_turned(t)
                        if pp is not None:
                            values_low(slab0 + (3 * pp - 1), (run.parity + pp) % 2)
                        if now and now[0] == "A":
                            max_of(1)
                        k = run.ends(t - 1)
                        if k is not None and k % 3 < 2:
                            slot = (run.parity + 1 + k // 3) % 2
                            part_low(slab0 + k, (q_lo, k_lo)[k % 3][:, slot], (q_hi, k_hi)[k % 3][:, slot], part[:])
                        k = run.weights_at(t)
                        if k is not None:
                            if not (run is RUN_CB and k >= 2):
                                split_proj(slab0 + (k + 2), (run.parity + k) % 2)
                            elif k == 3:
                                split_w(l, 1, 0, 0)
                        k = run.ends(t)
                        if k is not None:
                            evacuate(slab0 + k, pair0 + (1 + k // 3), k % 3, 1)

                with dve.Fori(0, 2) as a:
                    attend(RUN_A, STEPS * l + 16 * a, MAPS * l + 32 * a, 8 * a, 2 * a, 6 * a + 4)
                dve.wait_ge(o_rms, l + 1)
                V.reciprocal(o_inv[:], o_inv[:]).then_inc(o_inv_done, 1)
                dve.wait_ge(cum_out, 5 * l + 3)
                attend(RUN_C, STEPS * l + 32, MAPS * l + 64, 16, C0, 16)
                dve.wait_ge(cum_out, 5 * l + 5)
                attend(RUN_CB, STEPS * l + 48, MAPS * l + 80, 24, C0 + 1, 19)

                for n, c in enumerate(MIX_CHUNK):
                    dve.wait_ge(mix_hi_done, NC * l + n + 1)
                    V.scalar_tensor_tensor(out=mix_lo[:, c], in0=ps[2 + n % 2][:],
                                           scalar=mix_gain[:, bass.ds(NC * l + c, 1)],
                                           in1=mix_hi[:, c].bitcast(F32), op0=ALU.mult,
                                           op1=ALU.subtract).then_inc(mix_split, 1)

                def residual(mm, m, j):
                    r = result(l, 1, mm, j)
                    V.tensor_tensor(xt[:, 2 * m + j], r, xt[:, 2 * m + j], ALU.add).then_inc(evacuated, 1)

                def add_out(m, half):
                    for j in range(2):
                        split_w(l, 1, m + j, 1 - j)
                        dve.wait_ge(x_back[half], 16 * l + 16)
                        residual(m, m, j)
                        dve.wait_ge(h_hi_done, 2 * NC * l + 2 * m + (NC + j + 1))
                        V.scalar_tensor_tensor(out=h_lo[:, 2 * m + j], in0=xt[:, 2 * m + j],
                                               scalar=param[:, bass.ds(2 * NC * l + 2 * m + (NC + j), 1)],
                                               in1=h_hi[:, 2 * m + j].bitcast(F32), op0=ALU.mult,
                                               op1=ALU.subtract).then_inc(h_split, 1)

                for i in range(2):
                    with dve.Fori(NC // 4 * i, NC // 4 * (i + 1)) as m:
                        add_out(m, i)

                def hidden(g, m, j):
                    r = result(l, 1, NC * g + m + NC // 2, j)
                    V.scalar_tensor_tensor(out=ring[j][:], in0=r, scalar=0.0, in1=inv_rms[:], op0=ALU.max,
                                           op1=ALU.mult).then_inc(evacuated, 1)
                    dve.wait_ge(relu_sq, 4 * NC * l + NC * g + 2 * m + (j + 1))
                    V.tensor_tensor(u_lo[:, 2 * m + j], ring[j][:], u_hi[:, 2 * m + j].bitcast(F32),
                                    ALU.subtract).then_inc(u_split, 1)

                split_w(l, 1, NC // 2, 1)
                invert_rms(2 * l + 2)
                split_w(l, 1, NC // 2 + 1, 0)
                dve.wait_ge(rms_out, 2 * l + 2)
                hidden(0, 0, 0)
                hidden(0, 0, 1)

                def up(g, m):
                    for j in range(2):
                        split_w(l, 1, NC * g + m + (NC // 2 + j), 1 - j)
                        hidden(g, m, j)

                def down(g, m, last):
                    for j in range(2):
                        if not (last and isinstance(m, int) and j == 1):
                            split_w(l, 1, NC * g + m + (NC + j), 1 - j)
                        residual(NC * g + m + NC, m, j)
                        if last and not (isinstance(m, int) and j == 1):
                            dve.wait_ge(h_hi_done, 2 * NC * l + 2 * m + (2 * NC + j + 1))
                            V.scalar_tensor_tensor(out=h_lo[:, 2 * m + j], in0=xt[:, 2 * m + j],
                                                   scalar=param[:, bass.ds(2 * NC * l + 2 * m + (2 * NC + j), 1)],
                                                   in1=h_hi[:, 2 * m + j].bitcast(F32), op0=ALU.mult,
                                                   op1=ALU.subtract).then_inc(h_split, 1)

                with dve.Fori(1, NC // 2) as m:
                    up(0, m)
                with dve.Fori(0, NC // 2) as m:
                    down(0, m, False)
                with dve.Fori(1, GROUPS - 1) as g:
                    with dve.Fori(0, NC // 2) as m:
                        up(g, m)
                    with dve.Fori(0, NC // 2) as m:
                        down(g, m, False)
                with dve.Fori(0, NC // 2) as m:
                    up(GROUPS - 1, m)
                with dve.Fori(0, NC // 2 - 1) as m:
                    down(GROUPS - 1, m, True)
                down(GROUPS - 1, NC // 2 - 1, True)

            invert_rms(2 * DEPTH + 1)
            V.drain()
            for c in range(NC):
                dve.wait_ge(y_turned, NC * DEPTH + c + 1)
                V.tensor_tensor(rows[:, :, c * P:(c + 1) * P], ps[FINAL_PS[c % 3]][:].rearrange("p (b d) -> p b d", d=P),
                                rms_col[:].unsqueeze(2).to_broadcast([P, NQ, P]), ALU.mult).then_inc(rows_done, 1)

        @block.tensor
        def _(pe):
            def products(region, m, j, l, hi, lo, ready, count, between=None):
                pe.wait_ge(w_split, NSLAB * l + slab_no(region, m, j) + (1 + CREDIT))
                pe.wait_ge(evacuated, NSLAB * l + ring_free(region, m, j))
                pe.wait_ge(ready, count - 1)
                for c in range(NC):
                    if c == NC // 2 and between:
                        between()
                    if c == NC - 1:
                        pe.wait_ge(ready, count)
                    for n, (w, h) in enumerate(((w_hi, hi), (w_hi, lo), (w_lo, hi))):
                        for t in range(S // BANK):
                            mm = nc.tensor.matmul(ps[j][:, bass.ts(t, BANK)], w[:, j, c], h[:, c, bass.ts(t, BANK)],
                                                  start=(c == 0 and n == 0), stop=(c == NC - 1 and n == 2))
                mm.then_inc(slab_done, 1)

            def turn(src, dst, count, done):
                for b in range(count):
                    tr = nc.tensor.transpose(dst[:, b * P:(b + 1) * P], src[:, b * P:(b + 1) * P], ident[:])
                tr.then_inc(done, 1)

            def sum_squares(n):
                pe.wait_ge(sq_added, NC * n + (NC + CREDIT))
                for b in range(NQ):
                    mm = nc.tensor.matmul(ps[2][:, b:b + 1], sq_sum[:, b * P:(b + 1) * P], ones[:], start=True, stop=True)
                mm.then_inc(ss_done, 1)

            def spread_rms(n):
                pe.wait_ge(rms_inverted, n)
                for b in range(NQ):
                    mm = nc.tensor.matmul(ps[2][:, b * P:(b + 1) * P], rms_col[:, b:b + 1].to_broadcast([P, P]), ident[:],
                                          start=True, stop=True)
                mm.then_inc(rms_spread, 1)

            pe.sem_inc(slab_done, CREDIT)
            pe.sem_inc(turned, CREDIT)
            pe.wait_ge(setup_pool, 6)
            pe.wait_ge(par_loaded, 16 * (2 * DEPTH + 3))
            nc.tensor.transpose(ps[3][:, 0:64], par_raw[:], ident[0:64, 0:64]).then_inc(setup_pe, 1)
            for c in range(NC):
                if c % 2 == 0:
                    pe.wait_ge(x_loaded[c // 2], 16)
                if c >= 2:
                    pe.wait_ge(x_ready, c - 1)
                for b in range(NQ):
                    tr = nc.tensor.transpose(ps[c % 2][:, b * P:(b + 1) * P], rows[:, b, c * P:(c + 1) * P], ident[:])
                tr.then_inc(x_turned, 1)
            pe.wait_ge(x_ready, NC)

            with pe.Fori(0, DEPTH) as l:
                h_count = 2 * NC * l + NC

                def piece(s, j, p, c):
                    for n, (w, h) in enumerate(((w_hi, h_hi), (w_hi, h_lo), (w_lo, h_hi))):
                        for t in range(S // BANK):
                            mm = nc.tensor.matmul(ps[p][:, bass.ts(t, BANK)], w[:, j, c], h[:, c, bass.ts(t, BANK)],
                                                  start=(c == 0 and n == 0), stop=(c == NC - 1 and n == 2))
                    if c == NC - 1:
                        mm.then_inc(slab_done, 1)

                def project(s):
                    pe.wait_ge(w_split, NSLAB * l + s + (1 + CREDIT))
                    pe.wait_ge(evacuated, NSLAB * l + s - 1 + CREDIT)
                    if s:
                        pe.wait_ge(h_split, h_count)
                    for c in range(NC):
                        if s == 1 and c == NC // 2:
                            spread_rms(2 * l + 1)
                        if s == 0:
                            pe.wait_ge(h_split, 2 * NC * l + c + 1)
                        piece(s, s % 2, s % 2, c)

                def spread(head, p):
                    pick = ident[96:P, F_ROW + head:F_ROW + head + 1].to_broadcast([32, P])
                    for t in range(S // BANK):
                        mm = nc.tensor.matmul(ps[p][:, bass.ts(t, BANK)], pick, cum[96:P, bass.ts(t, BANK)],
                                              start=True, stop=True)
                    mm.then_inc(cum_ps, 1)

                project(0)
                sum_squares(2 * l)
                project(1)
                project(2)
                pe.wait_ge(cum_ready, l + 1)
                pe.wait_ge(rms_out, 2 * l + 1)
                spread(0, 3)
                for b in range(NQ):
                    tr = nc.tensor.transpose(ps[2][:, b * 32:(b + 1) * 32], cum[96:P, b * P:(b + 1) * P],
                                             ident[96:P, 96:P])
                tr.then_inc(cum_ps, 1)
                project(3)
                pe.wait_ge(cum_out, 5 * l + 2)
                spread(1, 2)
                pe.wait_ge(evacuated, NSLAB * l + (4 + CREDIT))
                turn(part, ps[1], NQ, v_turned)

                def scores(m0, n, qs, ks, i, j, k0, width, p0, read):
                    pe.wait_ge(scores_read, m0 + (read + CREDIT))
                    half = slice(j * HD, (j + 1) * HD)
                    for at in range(0, width, BANK):
                        w = min(BANK, width - at)
                        for p, (q, k) in enumerate(((q_hi, k_hi), (q_hi, k_lo), (q_lo, k_hi))):
                            mm = nc.tensor.matmul(ps[0][:, p0 + at:p0 + at + w], q[half, qs, i * P:(i + 1) * P],
                                                  k[half, ks, k0 * P + at:k0 * P + at + w],
                                                  start=(p == 0), stop=(p == 2))
                    mm.then_inc(scored, 1)

                def turn_probs(s0, t, slots, b0, blocks, early, ready, count):
                    pe.wait_ge(ready, count)
                    pe.wait_ge(pt_split, s0 + (t + (0 if early else 1)))
                    for k, slot in enumerate(slots):
                        for b in range(blocks):
                            at = (b0 + k * blocks + b) * P
                            tr = nc.tensor.transpose(ps[2][:, at:at + P], probs[:, slot, b * P:(b + 1) * P], ident[:])
                            if blocks > NQ // 2 and b == NQ // 2 - 1:
                                tr.then_inc(first_turned, 1)
                    tr.then_inc(turned, 1)

                def values(s0, t, slot, b0, k0, blocks, cols, wide):
                    if wide is None:
                        pe.wait_ge(pt_split, s0 + (t + 2))
                    else:
                        pe.wait_ge(first_split, WIDE * l + wide + 1)
                    pe.wait_ge(o_stored, s0 + (t - 1 + CREDIT))
                    at = BANK * (t % 2)
                    for k, (e0, e1) in enumerate(cols):
                        w = e1 - e0
                        o = ps[3][:, at:at + 2 * w]
                        for b in range(blocks):
                            if b == NQ // 2:
                                pe.wait_ge(pt_split, s0 + (t + 2))
                            nc.tensor.matmul(o.rearrange("p (h e) -> p h e", h=2), pt_hi[:, b0 + k * blocks + b],
                                             v_parts[:, slot, k0 + b, :, e0:e1], start=(b == 0), stop=False)
                            mm = nc.tensor.matmul(o[:, 0:w], pt_lo[:, b0 + k * blocks + b],
                                                  v_parts[:, slot, k0 + b, 0, e0:e1], start=False, stop=(b == blocks - 1))
                        at += 2 * w
                    mm.then_inc(pv_done, 1)

                def attend(run, s0, m0, w0, slab0):
                    def kv_slot(grp, pp):
                        return (run.parity + (1 if grp == "B" else pp)) % 2

                    def score(t, k):
                        grp, pp, i, j = run.steps[t]
                        k0, blocks = window(grp, i)
                        if run.pair_start[t] and k == 0:
                            pe.wait_ge(split_done, NPART * l + slab0 + (3 if grp == "B" and pp == 2 else 3 * pp - 2))
                        n = run.map0[t]
                        p0, read = (BANK * k, n) if grp == "B" else (0, n + k)
                        scores(m0, n + k, (run.parity + pp) % 2, kv_slot(grp, pp), i, k if j is None else j, k0,
                               blocks * P, p0, read)

                    def dense(pieces):
                        for k, c in pieces:
                            if c == 0:
                                s = slab0 + k
                                pe.wait_ge(w_split, NSLAB * l + s + (1 + CREDIT))
                                pe.wait_ge(evacuated, NSLAB * l + s + CREDIT)
                                if k % 3 == 0:
                                    pe.wait_ge(split_done, NPART * l + (s - 1))
                            piece(slab0 + k, (run.parity + k) % 2, 1, c)

                    def turn_step(u):
                        grp, pp, i, j = run.steps[u]
                        blocks, n, maps = window(grp, i)[1], run.map0[u], run.maps(u)
                        if grp == "A":
                            turn_probs(s0, u, [n % 4], 0, blocks, False, combined, s0 + (u + 1))
                        else:
                            turn_probs(s0, u, [n % 4, (n + 1) % 4][:maps], run.half(u), blocks, run.early(u),
                                       exp_done, m0 + (n + maps))

                    def values_step(u):
                        grp, pp, i, j = run.steps[u]
                        k0, blocks = window(grp, i)
                        if run.pair_start[u]:
                            pe.wait_ge(split_done, NPART * l + slab0 + (2 if grp == "B" and pp == 2 else 3 * pp - 1))
                        heads = [(0, HD), (HD, P)]
                        values(s0, u, kv_slot(grp, pp), run.half(u), k0, blocks,
                               [(0, P)] if grp == "A" else heads if grp == "B" else heads[j:j + 1], run.wide(w0, u))

                    for t in range(run.n + 2):
                        now = run.steps[t] if t < run.n else None
                        grp = now[0] if now else None
                        todo = list(run.pieces[t]) if t < len(run.pieces) else []
                        pp = run.values_turned(t)
                        if now:
                            score(t, 0)
                        if grp == "B":
                            score(t, 1)
                        if pp is not None:
                            pe.wait_ge(evacuated, NSLAB * l + slab0 + (3 * pp + CREDIT))
                            turn(part, ps[1], NQ, v_turned)
                        if t == run.n:
                            dense(todo)
                            todo = []
                        if grp in ("A", "C") and pp is None:
                            dense(todo[:1])
                            todo = todo[1:]
                        if run.early(t - 1):
                            dense(todo)
                            todo = []
                            turn_step(t - 1)
                        if t >= 2:
                            values_step(t - 2)
                        if grp == "A":
                            score(t, 1)
                        if grp == "A" and pp is None:
                            dense(todo[:1])
                            todo = todo[1:]
                        if run is RUN_A and t == 1:
                            pe.wait_ge(cum_out, 5 * l + 3)
                        if 1 <= t <= run.n and not run.early(t - 1):
                            turn_step(t - 1)
                        dense(todo)

                with pe.Fori(0, 2) as a:
                    attend(RUN_A, STEPS * l + 16 * a, MAPS * l + 32 * a, 8 * a, 6 * a + 4)
                attend(RUN_C, STEPS * l + 32, MAPS * l + 64, 16, 16)
                spread(2, 0)
                spread(3, 2)
                pe.wait_ge(cum_out, 5 * l + 5)
                attend(RUN_CB, STEPS * l + 48, MAPS * l + 80, 24, 19)

                def turn_out(n):
                    slab = [0, 1, 2, 3, B0, B0 + 1, C0, C0 + 1][MIX_CHUNK[n]]
                    if n == 0:
                        pe.wait_ge(o_scaled, AH * l + AH)
                    if n == 1:
                        pe.wait_ge(o_stored, STEPS * l + (STEPS + CREDIT))
                    if n >= 2:
                        pe.wait_ge(mix_split, NC * l + n - 1 + CREDIT)
                    turn(o_out[:, slab], ps[2 + n % 2], NQ, y_turned)

                turn_out(0)
                turn_out(1)
                pe.wait_ge(w_split, NSLAB * l + SPLIT + 1 + CREDIT)
                for k, c in enumerate(MIX_CHUNK):
                    pe.wait_ge(mix_split, NC * l + k + 1 + CREDIT)
                    for n, (w, h) in enumerate(((w_hi, mix_hi), (w_hi, mix_lo), (w_lo, mix_hi))):
                        for t in range(S // BANK):
                            mm = nc.tensor.matmul(ps[0][:, bass.ts(t, BANK)], w[:, 0, c], h[:, c, bass.ts(t, BANK)],
                                                  start=(k == 0 and n == 0), stop=(k == NC - 1 and n == 2))
                    if k + 2 < NC:
                        turn_out(k + 2)
                mm.then_inc(slab_done, 1)
                products(1, 0, 1, l, mix_hi, mix_lo, mix_split, NC * l + (NC + CREDIT))
                with pe.Fori(1, NOUT // 2) as m:
                    for j in range(2):
                        products(1, m, j, l, mix_hi, mix_lo, mix_split, NC * l + (NC + CREDIT))

                def up(g, m, j, between=None):
                    products(1, NC * g + m + NC // 2, j, l, h_hi, h_lo, h_split, h_count + NC, between)

                def down(g, m, j):
                    products(1, NC * g + m + NC, j, l, u_hi, u_lo, u_split, 4 * NC * l + NC * g + NC)

                up(0, 0, 0)
                sum_squares(2 * l + 1)
                up(0, 0, 1, lambda: spread_rms(2 * l + 2))
                with pe.Fori(1, NC // 2) as m:
                    for j in range(2):
                        up(0, m, j)
                with pe.Fori(0, NC // 2) as m:
                    for j in range(2):
                        down(0, m, j)
                with pe.Fori(1, GROUPS) as g:
                    with pe.Fori(0, NC // 2) as m:
                        for j in range(2):
                            up(g, m, j)
                    with pe.Fori(0, NC // 2) as m:
                        for j in range(2):
                            down(g, m, j)

            for c in range(NC):
                if c == 2:
                    sum_squares(2 * DEPTH)
                pe.wait_ge(y_ready, c + 1)
                if c >= 3:
                    pe.wait_ge(rows_done, c - 2)
                turn(turn_in[c % 2], ps[FINAL_PS[c % 3]], NQ, y_turned)


_INS = ["x", "w_in", "a_lambda", "a_subln", "b_sinks", "c_fbias", "w_out", "g_mix", "g_mlp", "w_up", "w_down", "g_final"]


def kernel(**inputs):
    import concourse.bacc as _bacc
    from concourse.bass_utils import run_bass_kernel_spmd as _run

    nc = _bacc.Bacc("TRN2", target_bir_lowering=False, num_devices=1)
    arrays, args = {}, []
    for name in _INS:
        a = np.ascontiguousarray(inputs[name])
        arrays[f"in_{name}_dram"] = a
        args.append(nc.dram_tensor(f"in_{name}_dram", a.shape, mybir.dt.from_np(a.dtype), kind="ExternalInput").ap())
    shape = inputs["x"].shape
    args.append(nc.dram_tensor("out_0_dram", shape, F32, kind="ExternalOutput").ap())
    hybrid_encoder(nc, *args)
    r = _run(nc, [arrays], core_ids=[0])
    return r.results[0]["out_0_dram"]
```
